# Optimizing a Trainium2 kernel written in Bass

```python
import math
import jax, jax.numpy as jnp
from jax import lax
import numpy as np

D_MODEL = 1024
BATCH = 1
SEQ = 1024
DEPTH = 1

POOL_WINDOWS = (2, 4, 8, 16)
POOL_GROUPS = len(POOL_WINDOWS)
POOL_WIDTH = D_MODEL
POOL_GROUP_DIM = POOL_WIDTH // POOL_GROUPS
SSM_EXPAND = 2
SSM_INNER = SSM_EXPAND * D_MODEL
SSM_HEAD_DIM = 64
SSM_HEADS = SSM_INNER // SSM_HEAD_DIM
SSM_GROUPS = 8
SSM_HEADS_PER_GROUP = SSM_HEADS // SSM_GROUPS
SSM_STATE = 128
SSM_CONV = 4
SSM_CHUNK = 128
SSM_CONV_DIM = SSM_INNER + 2 * SSM_GROUPS * SSM_STATE
SSM_NORM_GROUP = SSM_INNER // SSM_GROUPS
N_BRANCHES = 2
SPLITS = (
    POOL_WIDTH,
    POOL_WIDTH + SSM_INNER,
    POOL_WIDTH + SSM_INNER + SSM_CONV_DIM,
    POOL_WIDTH + SSM_INNER + SSM_CONV_DIM + SSM_HEADS,
    POOL_WIDTH + SSM_INNER + SSM_CONV_DIM + SSM_HEADS + D_MODEL,
)
IN_COLS = POOL_WIDTH + SSM_INNER + SSM_CONV_DIM + SSM_HEADS + N_BRANCHES * D_MODEL
PEER_HEADS = 8
PEER_KEYS = 128
PEER_EXPERTS = PEER_KEYS * PEER_KEYS
PEER_QUERY = 256
PEER_HALF = PEER_QUERY // 2
PEER_TOPK = 16
PEER_BLOCK = 128
DN_ALPHA = (2.0 * DEPTH) ** 0.25
DN_BETA = (8.0 * DEPTH) ** -0.25
LN_EPS = 1e-5
RMS_EPS = 1e-5

kernel_name = "hybrid_pool_ssd_peer_deepnorm"

def layer_norm(x, g, b):
    xf = x.astype(jnp.float32)
    mu = jnp.mean(xf, axis=-1, keepdims=True)
    xc = xf - mu
    var = jnp.mean(xc * xc, axis=-1, keepdims=True)
    return (xc * lax.rsqrt(var + LN_EPS) * g.astype(jnp.float32) + b.astype(jnp.float32)).astype(x.dtype)

def pool_mixer(u, pool_w, pool_scale):
    b, l, _ = u.shape
    uf = u.astype(jnp.float32).reshape(b, l, POOL_GROUPS, POOL_GROUP_DIM)
    cs = jnp.cumsum(uf, axis=1)
    pos = jnp.arange(1, l + 1, dtype=jnp.float32)
    means = []
    for gi, w in enumerate(POOL_WINDOWS):
        c = cs[:, :, gi]
        lagged = jnp.pad(c, ((0, 0), (w, 0), (0, 0)))[:, :l]
        count = jnp.minimum(pos, float(w))[None, :, None]
        means.append((c - lagged) / count)
    pooled = jnp.stack(means, axis=2) - uf
    mixed = jnp.einsum('blgc,gcd->blgd', pooled, pool_w.astype(jnp.float32))
    return (mixed.reshape(b, l, POOL_WIDTH) * pool_scale.astype(jnp.float32)).astype(u.dtype)

def causal_depthwise_conv(v, w, bias):
    out = lax.conv_general_dilated(
        v, w[:, None, :], window_strides=(1,), padding=[(SSM_CONV - 1, 0)],
        dimension_numbers=('NWC', 'WIO', 'NWC'), feature_group_count=v.shape[-1])
    return out + bias

def seg_decay(acum):
    q = acum.shape[-1]
    mask = jnp.tril(jnp.ones((q, q), dtype=bool))
    diff = acum[..., :, None] - acum[..., None, :]
    return jnp.exp(jnp.where(mask, diff, -jnp.inf))

def ssd_scan(x, dt, a, bmat, cmat):
    b, l = x.shape[0], x.shape[1]
    nc = l // SSM_CHUNK
    G, R, P, N, Q = SSM_GROUPS, SSM_HEADS_PER_GROUP, SSM_HEAD_DIM, SSM_STATE, SSM_CHUNK
    xd = (x.astype(jnp.float32) * dt[..., None]).reshape(b, nc, Q, G, R, P)
    adt = (dt * a).reshape(b, nc, Q, G, R)
    acum = jnp.cumsum(adt, axis=2).transpose(0, 1, 3, 4, 2)
    bc = bmat.astype(jnp.float32).reshape(b, nc, Q, G, N)
    cc = cmat.astype(jnp.float32).reshape(b, nc, Q, G, N)
    lmat = seg_decay(acum)
    cb = jnp.einsum('bclgn,bcsgn->bcgls', cc, bc)
    y_diag = jnp.einsum('bcgls,bcgrls,bcsgrp->bclgrp', cb, lmat, xd)
    decay_states = jnp.exp(acum[..., -1:] - acum)
    states = jnp.einsum('bclgn,bcgrl,bclgrp->bcgrpn', bc, decay_states, xd)
    chunk_decay = jnp.exp(acum[..., -1])

    def step(h, inp):
        st, dc = inp
        return h * dc[..., None, None] + st, h

    h0 = jnp.zeros((b, G, R, P, N), jnp.float32)
    _, prev = lax.scan(step, h0, (jnp.moveaxis(states, 1, 0), jnp.moveaxis(chunk_decay, 1, 0)))
    prev = jnp.moveaxis(prev, 0, 1)
    y_off = jnp.einsum('bclgn,bcgrpn,bcgrl->bclgrp', cc, prev, jnp.exp(acum))
    return (y_diag + y_off).reshape(b, l, SSM_HEADS, P)

def ssm_mixer(z, xbc, dt_raw, conv_w, conv_b, dt_bias, a_log, d_skip, norm_w, out_w):
    b, l, _ = z.shape
    xbc = jax.nn.silu(causal_depthwise_conv(xbc, conv_w, conv_b))
    xs = xbc[..., :SSM_INNER].reshape(b, l, SSM_HEADS, SSM_HEAD_DIM)
    bm = xbc[..., SSM_INNER:SSM_INNER + SSM_GROUPS * SSM_STATE].reshape(b, l, SSM_GROUPS, SSM_STATE)
    cm = xbc[..., SSM_INNER + SSM_GROUPS * SSM_STATE:].reshape(b, l, SSM_GROUPS, SSM_STATE)
    dt = jax.nn.softplus(dt_raw.astype(jnp.float32) + dt_bias.astype(jnp.float32))
    a = -jnp.exp(a_log.astype(jnp.float32))
    y = ssd_scan(xs, dt, a, bm, cm)
    y = y + d_skip.astype(jnp.float32)[:, None] * xs.astype(jnp.float32)
    y = y.reshape(b, l, SSM_INNER) * jax.nn.silu(z.astype(jnp.float32))
    yg = y.reshape(b, l, SSM_GROUPS, SSM_NORM_GROUP)
    yg = yg * lax.rsqrt(jnp.mean(yg * yg, axis=-1, keepdims=True) + RMS_EPS)
    y = (yg.reshape(b, l, SSM_INNER) * norm_w.astype(jnp.float32)).astype(z.dtype)
    return y @ out_w

def peer(x, w_q, sub_keys, expert_u, expert_v):
    b, l, d = x.shape
    t = b * l
    xt = x.reshape(t, d)
    q = (xt @ w_q).reshape(t, PEER_HEADS, 2, PEER_HALF).astype(jnp.float32)
    s = jnp.einsum('thkc,knc->thkn', q, sub_keys.astype(jnp.float32))
    top_s, top_i = lax.top_k(s, PEER_TOPK)
    cand_s = top_s[:, :, 0, :, None] + top_s[:, :, 1, None, :]
    cand_i = top_i[:, :, 0, :, None] * PEER_KEYS + top_i[:, :, 1, None, :]
    best_s, best_pos = lax.top_k(cand_s.reshape(t, PEER_HEADS, PEER_TOPK * PEER_TOPK), PEER_TOPK)
    expert_idx = jnp.take_along_axis(cand_i.reshape(t, PEER_HEADS, PEER_TOPK * PEER_TOPK), best_pos, axis=-1)
    gate = jax.nn.softmax(best_s, axis=-1)
    nb = t // PEER_BLOCK

    def block(args):
        xb, ib, gb = args
        h = jnp.einsum('td,thkd->thk', xb, expert_u[ib])
        act = (jax.nn.gelu(h.astype(jnp.float32), approximate=False) * gb).astype(xb.dtype)
        return jnp.einsum('thk,thkd->td', act, expert_v[ib])

    out = lax.map(block, (xt.reshape(nb, PEER_BLOCK, d),
                          expert_idx.reshape(nb, PEER_BLOCK, PEER_HEADS, PEER_TOPK),
                          gate.reshape(nb, PEER_BLOCK, PEER_HEADS, PEER_TOPK)))
    return out.reshape(b, l, d)

def setup_inputs(seed: int = 0) -> dict:
    key = jax.random.key(seed)
    ks = jax.random.split(key, 20)
    f32 = jnp.float32
    nrm = lambda k, shape, scale: jax.random.normal(k, shape, f32) * scale
    dt0 = jnp.exp(jax.random.uniform(ks[6], (DEPTH, SSM_HEADS), f32)
                  * (math.log(0.1) - math.log(0.001)) + math.log(0.001))
    return {
        "x": nrm(ks[0], (BATCH, SEQ, D_MODEL), 1.0),
        "w_in": nrm(ks[1], (DEPTH, D_MODEL, IN_COLS), D_MODEL ** -0.5),
        "pool_w": nrm(ks[2], (DEPTH, POOL_GROUPS, POOL_GROUP_DIM, POOL_GROUP_DIM), POOL_GROUP_DIM ** -0.5),
        "pool_scale": 1.0 + nrm(ks[3], (DEPTH, POOL_WIDTH), 0.02),
        "conv_w": nrm(ks[4], (DEPTH, SSM_CONV, SSM_CONV_DIM), SSM_CONV ** -0.5),
        "conv_b": nrm(ks[5], (DEPTH, SSM_CONV_DIM), 0.02),
        "dt_bias": dt0 + jnp.log(-jnp.expm1(-dt0)),
        "a_log": jnp.log(jax.random.uniform(ks[7], (DEPTH, SSM_HEADS), f32, 1.0, 16.0)),
        "d_skip": 1.0 + nrm(ks[8], (DEPTH, SSM_HEADS), 0.02),
        "ssm_norm_w": 1.0 + nrm(ks[9], (DEPTH, SSM_INNER), 0.02),
        "ssm_out": nrm(ks[10], (DEPTH, SSM_INNER, D_MODEL), SSM_INNER ** -0.5),
        "w_out": nrm(ks[11], (DEPTH, D_MODEL, D_MODEL), D_MODEL ** -0.5 * DN_BETA),
        "ln1_g": 1.0 + nrm(ks[12], (DEPTH, D_MODEL), 0.02),
        "ln1_b": nrm(ks[13], (DEPTH, D_MODEL), 0.02),
        "w_q": nrm(ks[14], (DEPTH, D_MODEL, PEER_HEADS * PEER_QUERY), D_MODEL ** -0.5),
        "sub_keys": nrm(ks[15], (DEPTH, 2, PEER_KEYS, PEER_HALF), PEER_HALF ** -0.5),
        "expert_u": nrm(ks[16], (DEPTH, PEER_EXPERTS, D_MODEL), D_MODEL ** -0.5),
        "expert_v": nrm(ks[17], (DEPTH, PEER_EXPERTS, D_MODEL), DN_BETA),
        "ln2_g": 1.0 + nrm(ks[18], (DEPTH, D_MODEL), 0.02),
        "ln2_b": nrm(ks[19], (DEPTH, D_MODEL), 0.02),
    }

def reference(x, w_in, pool_w, pool_scale, conv_w, conv_b, dt_bias, a_log, d_skip, ssm_norm_w,
              ssm_out, w_out, ln1_g, ln1_b, w_q, sub_keys, expert_u, expert_v, ln2_g, ln2_b):
    h = x
    for i in range(DEPTH):
        proj = h @ w_in[i]
        pool_in, z, xbc, dt_raw, g_pool, g_ssm = jnp.split(proj, SPLITS, axis=-1)
        a_out = pool_mixer(pool_in, pool_w[i], pool_scale[i])
        m_out = ssm_mixer(z, xbc, dt_raw, conv_w[i], conv_b[i], dt_bias[i], a_log[i],
                          d_skip[i], ssm_norm_w[i], ssm_out[i])
        merged = jax.nn.sigmoid(g_pool) * a_out + jax.nn.sigmoid(g_ssm) * m_out
        h = layer_norm(DN_ALPHA * h + merged @ w_out[i], ln1_g[i], ln1_b[i])
        h = layer_norm(DN_ALPHA * h + peer(h, w_q[i], sub_keys[i], expert_u[i], expert_v[i]),
                       ln2_g[i], ln2_b[i])
    return h


_drawn_inputs = setup_inputs


def setup_inputs(seed=0):
    import zlib

    import numpy as np

    out = dict(_drawn_inputs(seed))
    spreads = {}
    factors = {'pool_scale': 3.237, 'd_skip': 3.517, 'ssm_norm_w': 2.791, 'ln2_g': 2.907, 'ln2_b': 2.842}
    for name, (base, spread) in spreads.items():
        noise = np.random.default_rng([zlib.crc32(name.encode()), seed]).standard_normal(out[name].shape)
        drawn = base * np.exp(spread * noise) if base else spread * noise
        out[name] = __import__('jax').numpy.asarray(drawn.astype(out[name].dtype))
    for name, factor in factors.items():
        out[name] = (out[name] * factor).astype(out[name].dtype)
    return out
```

```python
from contextlib import ExitStack

import concourse.bass as bass
from concourse import mybir

ALU = mybir.AluOpType
ACT = mybir.ActivationFunctionType
AX = mybir.AxisListType
F32 = mybir.dt.float32
U32 = mybir.dt.uint32
ds = bass.ds

P = 128
SEQ = 1024
D = 1024
KD = D // P
T = 256
NT = T // P
NC = SEQ // T
WINDOWS = (2, 4, 8, 16)
HALO = 16
INNER = 2 * D
HEADS = 32
HD = 64
GROUPS = 8
HG = HEADS // GROUPS
GW = HG * HD
TAPS = 4
PH = 8
KEYS = 128
TOPK = 16
UNITS = NT * PH
NCAND = sum(TOPK // (i + 1) for i in range(TOPK))
ALPHA = 2.0 ** 0.25
EPS = 1e-5
NEG = -1e30
LOWEST = -3.4028234663852886e38

RING = 4
AJ = 4
BA, BC, BW, BD = 8 * AJ, 12, 4, 8
BLOCKS = BA + BC + BW + BD
MA, MC, MW, MD = 8, 8, 4, 8
MAINS = AJ * MA + MC + MW + MD
TA, TW, TD = 6, 4, 8
TURNS = AJ * TA + TW + TD
ROWS = 8


def build(nc, x, xt, wblocks, wdt, poolw, pscale, convw, convb, dtb, alog, dskip, normw,
          ln1g, ln1b, ln2g, ln2b, subkt, eu, ev, out):
    with ExitStack() as ctx:
        def sb(name, shape, dt=F32):
            return ctx.enter_context(nc.sbuf_tensor(name, shape, dt))

        def pb(name):
            return ctx.enter_context(nc.psum_tensor(name, [P, 512], F32))

        def sem(name):
            return ctx.enter_context(nc.semaphore(name))

        main = pb("main0"), pb("main1")
        turn = pb("turn0"), pb("turn1")
        lbank = pb("lbank")
        cbbank = pb("cbbank")
        ybank = pb("ybank")
        stbank = pb("stbank")

        ring = [sb(f"ring{r}", [P, KD, 256]) for r in range(RING)]
        xT = sb("xT", [P, KD, T])
        pw = sb("pw", [P, 2, 256])
        wdt_s = sb("wdt_s", [P, KD, HEADS])
        subk = sb("subk", [P, 2, KEYS])
        lng1, lnb1 = sb("lng1", [P, D]), sb("lnb1", [P, D])
        lng2, lnb2 = sb("lng2", [P, D]), sb("lnb2", [P, D])
        cw = sb("cw", [P, AJ * 4 * 2, TAPS])
        cbias = sb("cbias", [P, AJ * 4 * 2])
        psc = sb("psc", [P, KD])
        nw = sb("nw", [P, INNER // P])
        dtb_s, a_s, dsk = sb("dtb_s", [P, HEADS]), sb("a_s", [P, HEADS]), sb("dsk", [P, HEADS])
        ident, upper, ones = sb("ident", [P, P]), sb("upper", [P, P]), sb("ones", [P, P])
        mask = sb("mask", [P, HG, P])
        iota = sb("iota", [P, NCAND])
        pcoef = sb("pcoef", [P, 4, 4])
        pfix = sb("pfix", [P, 4, 16])
        craw = sb("craw", [P, 2, 2, 3 + T])
        cout = sb("cout", [P, 2, 2, T])
        ctail = sb("ctail", [P, AJ * 4 * 2, 3])
        early = sb("early", [P, 2 * KD * P])
        xs = early[:, 0:4 * T].rearrange("p (c t) -> p c t", c=4)
        xtok = early[:, 4 * T:4 * T + NT * 512].rearrange("p (t c) -> p t c", t=NT)
        hT = early[:, :].rearrange("p (k t) -> p k t", k=KD)
        BT, CT = sb("BT", [P, 2, T]), sb("CT", [P, 2, T])
        btok = sb("btok", [P, NT, 256])
        zy = sb("zy", [P, 2 * NT * 512])
        zs = zy[:, 0:NT * 512].rearrange("p (t c) -> p t c", t=NT)
        yg = zy[:, NT * 512:].rearrange("p (t c) -> p t c", t=NT)
        xres = zy[:, :].rearrange("p (t c) -> p t c", t=NT)
        praw = sb("praw", [P, 2, HALO + T])
        ptail = sb("ptail", [P, KD, HALO])
        pooled = sb("pooled", [P, 2, T])
        merged = sb("merged", [P, KD, T])
        state = sb("state", [P, INNER])
        lexp = sb("lexp", [P, 2, HG, P])
        gps, asb = (lexp[:, b, :, :].rearrange("p h l -> p (h l)").rearrange("p (a t) -> p a t", a=2) for b in range(2))
        mm = sb("mm", [P, 2, HG, P])
        scr = sb("scr", [P, 4 * (HALO + T)])
        psa, psb = (scr[:, a * 2 * (HALO + T):(a + 1) * 2 * (HALO + T)].rearrange("p (a t) -> p a t", a=2) for a in range(2))
        xd, xdd = (scr[:, a * 2 * GW:(a + 1) * 2 * GW].rearrange("p (b n) -> p b n", b=2) for a in range(2))
        yt1, yt2 = sb("yt1", [P, GW]), sb("yt2", [P, GW])
        NTH = NT * HEADS
        dtv, dte, dtu, dtl = sb("dtv", [P, NTH]), sb("dte", [P, NTH]), sb("dtu", [P, NTH]), sb("dtl", [P, NTH])
        dt_ = sb("dt_", [P, NTH])
        adt = sb("adt", [P, NTH])
        adtc = sb("adtc", [P, NT, 2 * HG])
        nacum, eacum, dst, cdec = (sb(n, [P, NTH]) for n in ("nacum", "eacum", "dst", "cdec"))
        rms = sb("rms", [P, 4])
        rmsr = sb("rmsr", [P, 4])
        late = sb("late", [P, INNER // P * T])
        yT = late[:, :].rearrange("p (k t) -> p k t", k=INNER // P)
        qT = late[:, 0:1024].rearrange("p (b s t) -> p b s t", b=2, s=2)
        ssb = late[:, 1024:2048].rearrange("p (b r n) -> p b r n", b=2, r=4)
        sel1 = late[:, 2048:2048 + TOPK * NCAND].rearrange("p (k n) -> p k n", k=TOPK)
        snext = late[:, 2848:2848 + KEYS]
        bm = late[:, 2976:2976 + 128].rearrange("p (u k) -> p u k", u=8)
        posf = late[:, 3104:3104 + 128].rearrange("p (u k) -> p u k", u=8)
        self_ = late[:, 3232:3232 + 128].rearrange("p (u k) -> p u k", u=8)
        bex = late[:, 3360:3360 + 128].rearrange("p (u k) -> p u k", u=8)
        bsum = late[:, 3488:3488 + 8]
        cnext = late[:, 3496:3496 + NCAND]
        mflat = merged[:, :, :].rearrange("p k t -> p (k t)")
        tm = mflat[:, 0:256].rearrange("p (u s k) -> p u s k", u=8, s=2)
        tf = mflat[:, 256:512].rearrange("p (u s k) -> p u s k", u=8, s=2)
        cand = mflat[:, 512:512 + 8 * NCAND].rearrange("p (u n) -> p u n", u=8)
        candi = mflat[:, 912:912 + 8 * NCAND].rearrange("p (u n) -> p u n", u=8)
        tmi = sb("tmi", [P, 8, 2, TOPK], U32)
        pos = sb("pos", [P, 8, TOPK], U32)
        hf = sb("hf", [P, NT, D])
        stats, mv = sb("stats", [P, NT, 2, 6]), sb("mv", [P, NT, 2])
        lstd = sb("lstd", [P, NT])
        lrst = sb("lrst", [P, NT])
        idxf, gatef = sb("idxf", [P, UNITS, TOPK], U32), sb("gatef", [P, UNITS, TOPK])
        idxp, gatep = sb("idxp", [P, UNITS + 1, TOPK], U32), sb("gatep", [P, UNITS, TOPK])
        hp = sb("hp", [P, NT, D])
        icur = [sb(f"icur{b}", [P, TOPK], U32) for b in range(2)]
        hdot, hgel, hact = (sb(n, [P, 2, TOPK]) for n in ("hdot", "hgel", "hact"))
        rows = [sb(f"rows{r}", [P, D]) for r in range(ROWS)]
        acc = sb("acc", [P, D])
        pstats, pmv = sb("pstats", [P, 2, 6]), sb("pmv", [P, 2])
        pstd, prst = sb("pstd", [P, 1]), sb("prst", [P, 1])

        const_dma = sem("const_dma")
        const_made = sem("const_made")
        dve_ready = sem("dve_ready")
        a_made = sem("a_made")
        w_ready = [sem(f"w_ready{r}") for r in range(RING)]
        block_done = sem("block_done")
        xt_ready = sem("xt_ready")
        pw_ready = sem("pw_ready")
        xres_ready = sem("xres_ready")
        main_free = sem("main_free")
        turn_ready = sem("turn_ready")
        turn_free = sem("turn_free")
        conv_raw, conv_out, conv_act = sem("conv_raw"), sem("conv_out"), sem("conv_act")
        pool_raw, pool_done = sem("pool_raw"), sem("pool_done")
        dt_proj, dt_abs, dt_exp, dt_u, dt_ln = (sem(n) for n in ("dt_proj", "dt_abs", "dt_exp", "dt_u", "dt_ln"))
        adt_ready, acum_ready, dec_in, dec_ready = (sem(n) for n in ("adt_ready", "acum_ready", "dec_in", "dec_ready"))
        adtc_ready = sem("adtc_ready")
        l_ready, lexp_ready = sem("l_ready"), sem("lexp_ready")
        cb_ready, m_done = sem("cb_ready"), sem("m_done")
        y_ready, y_free, st_ready, st_used = sem("y_ready"), sem("y_free"), sem("st_ready"), sem("st_used")
        rms_in, rms_sqrt, rms_rstd = sem("rms_in"), sem("rms_sqrt"), sem("rms_rstd")
        yn_ready = sem("yn_ready")
        pair_merged = sem("pair_merged")
        ln1_var, ln1_std, h_ready = sem("ln1_var"), sem("ln1_std"), sem("h_ready")
        topk_done = sem("topk_done")
        sm_in, sm_exp = sem("sm_in"), sem("sm_exp")
        idx_ready = sem("idx_ready")
        row_ready = [sem(f"row_ready{r}") for r in range(ROWS)]
        row_free = sem("row_free")
        gelu_ready = sem("gelu_ready")
        ln2_var, ln2_std, out_ready, out_done = (sem(n) for n in ("ln2_var", "ln2_std", "out_ready", "out_done"))

        BANKS = 2
        CONV = 2
        TURNED = 3
        LEXP = STATE = 1
        NCONST = 12

        def spread(ap, n):
            s = list(ap.shape)
            return ap.unsqueeze(len(s)).to_broadcast(s + [n])

        def heads(table, t, j, gg):
            return table[:, ds(t * HEADS + j * 2 * HG + gg * HG, HG)]

        def weave(slots, front, per_slot=1):
            for _ in slots:
                for _ in range(per_slot):
                    next(front, None)
            for _ in front:
                pass

        def emptied(eng, c, m):
            eng.wait_ge(main_free, c * MAINS + m + BANKS)

        def unturned(eng, c, m):
            eng.wait_ge(turn_free, c * TURNS + m + BANKS)

        block = ctx.enter_context(nc.Block())

        @block.sync
        def _(sp):
            for dst_, src in ((wdt_s[:, :, :], wdt), (subk[:, :, :], subkt), (cw[:, :, :], convw),
                              (cbias[:, :], convb), (psc[:, :], pscale), (nw[:, :], normw),
                              (dtb_s[:, :], dtb.to_broadcast([P, HEADS])),
                              (a_s[:, :], alog.to_broadcast([P, HEADS])),
                              (dsk[:, :], dskip.to_broadcast([P, HEADS])),
                              (lng1[:, :], ln1g.to_broadcast([P, D])), (lnb1[:, :], ln1b.to_broadcast([P, D])),
                              (lng2[:, :], ln2g.to_broadcast([P, D]))):
                sp.dma_start(dst_, src).then_inc(const_dma, 16)

            def load_blocks(c, b):
                for r in range(RING):
                    sp.wait_ge(block_done, c * BLOCKS + b + r + 1)
                    sp.dma_start(ring[r][:, :, :], wblocks[ds(b + r, 1), :, :].rearrange("o p (k n) -> (o p) k n", k=KD)
                                 ).then_inc(w_ready[r], 16)

            def load_xt(c):
                sp.dma_start(xT[:, :, :], xt[:, :, ds(c * T, T)]).then_inc(xt_ready, 16)

            def superchunk(c):
                with sp.Fori(0, AJ) as j:
                    load_blocks(c, j * 8)
                    sp.wait_ge(turn_ready, c * TURNS + (j - 1) * TA + 4 + TURNED)
                    sp.dma_start(pw[:, :, :], poolw[ds(j, 1), :, :, :].rearrange("o p k n -> (o p) k n")
                                 ).then_inc(pw_ready, 16)
                    load_blocks(c, j * 8 + 4)
                with sp.Fori(0, 2) as m:
                    load_blocks(c, BA + m * 4)
                sp.wait_ge(turn_ready, c * TURNS + AJ * TA + TURNED)
                sp.dma_start(xres, x[ds(c * T, T), :].rearrange("(t p) d -> p t d", p=P)).then_inc(xres_ready, 16)
                with sp.Fori(0, 4) as m:
                    load_blocks(c, BA + 8 + m * 4)

            load_xt(0)
            with sp.Fori(0, NC - 1) as c:
                superchunk(c)
                load_xt(c + 1)
            superchunk(NC - 1)

        @block.gpsimd
        def _(pool):
            pool.memset(ones[:, :], 1.0).then_inc(const_made, 1)
            pool.memset(mask[:, :, :], 0.0).then_inc(const_made, 1)
            pool.wait_ge(const_dma, 16 * NCONST)
            pool.memset(ident[:, :], 0.0).then_inc(const_made, 1)
            pool.wait_ge(const_made, 3)
            pool.affine_select(out=ident[:, :], in_=ident[:, :], compare_op=ALU.not_equal, fill=1.0, base=0,
                               pattern=[[1, P]], channel_multiplier=-1).then_inc(const_made, 1)
            pool.affine_select(out=upper[:, :], in_=ones[:, :], compare_op=ALU.is_ge, fill=0.0, base=0,
                               pattern=[[1, P]], channel_multiplier=-1).then_inc(const_made, 1)
            pool.affine_select(out=mask[:, :, :], in_=mask[:, :, :], compare_op=ALU.is_ge, fill=NEG, base=0,
                               pattern=[[0, HG], [1, P]], channel_multiplier=-1).then_inc(const_made, 1)
            pool.iota(iota[:, :], pattern=[[1, NCAND]], base=0, channel_multiplier=0,
                      allow_small_or_imprecise_dtypes=True).then_inc(const_made, 1)
            for w in range(4):
                pool.iota(pfix[:, w, :], pattern=[[1, 16]], base=1, channel_multiplier=0,
                          allow_small_or_imprecise_dtypes=True).then_inc(const_made, 1)

            count = pool.alloc_register("gathers_issued")
            pool.reg_mov(count, 1)
            with pool.Fori(0, NC * UNITS // 2) as pair:
                for b in range(2):
                    for table in (eu, ev):
                        for k in range(TOPK):
                            n = pool.snap(count)
                            if table is eu and k == 0:
                                pool.wait_ge(idx_ready, pair * 2 + b + 1)
                            pool.wait_ge(row_free, n)
                            pool.reg_add(count, count, 1)
                            pool.indirect_dma_start(rows[k % ROWS][:, :], None, table,
                                                    bass.IndirectOffsetOnAxis(ap=icur[b][:, k:k + 1], axis=0)
                                                    ).then_inc(row_ready[k % ROWS], 16)

        @block.tensor
        def _(pe):
            def block_in(c, turns, n):
                pe.wait_ge(w_ready[n % RING], (c * (BLOCKS // RING) + turns + n // RING + 1) * 16)
                return ring[n % RING]

            def bank(c, m, n):
                pe.wait_ge(main_free, c * MAINS + m + n + 1)
                return main[n % 2]

            def turn_bank(c, m, n):
                pe.wait_ge(turn_free, c * TURNS + m + n + 1)
                return turn[n % 2]

            def channels(dst_, w, src):
                for ct in range(2):
                    for k in range(KD):
                        last = pe.matmul(dst_[:, ct * T:(ct + 1) * T], w[:, k, ct * P:(ct + 1) * P], src[:, k, :],
                                         start=(k == 0), stop=(k == KD - 1))
                return last

            def tokens(dst_, w, src):
                for t in range(NT):
                    for k in range(KD):
                        last = pe.matmul(dst_[:, t * 256:(t + 1) * 256], src[:, k, t * P:(t + 1) * P], w[:, k, :],
                                         start=(k == 0), stop=(k == KD - 1))
                return last

            def dt_stage(c):
                pe.wait_ge(st_used, c * 4 * AJ + STATE)
                for t in range(NT):
                    for k in range(KD):
                        last = pe.matmul(stbank[:, 256 + t * HEADS:256 + (t + 1) * HEADS], xT[:, k, t * P:(t + 1) * P],
                                         wdt_s[:, k, :], start=(k == 0), stop=(k == KD - 1))
                last.then_inc(dt_proj, 1)
                pe.wait_ge(adt_ready, c + 1)
                pe.matmul(stbank[:, 320:320 + NTH], upper[:, :], adt[:, :], start=True, stop=True)
                pe.matmul(stbank[:, 384:384 + NTH], ones[:, :], adt[:, :], start=True, stop=True).then_inc(acum_ready, 1)

            def scan_scores(c, j, s):
                t, gg = s // 2, s % 2
                n = c * 4 * AJ + j * 4 + s
                pe.wait_ge(m_done, n + 2)
                pe.matmul(cbbank[:, 0:P], BT[:, gg, t * P:(t + 1) * P], CT[:, gg, t * P:(t + 1) * P],
                          start=True, stop=True).then_inc(cb_ready, 1)
                pe.wait_ge(lexp_ready, n + LEXP)
                pe.matmul(lbank[:, :], ident[:, :], mask[:, :, :].rearrange("p h l -> p (h l)"), start=True, stop=False,
                          skip_group_check=True)
                for h in range(HG):
                    last = pe.matmul(lbank[:, h * P:(h + 1) * P],
                                     adtc[:, t, gg * HG + h:gg * HG + h + 1].to_broadcast([P, P]), upper[:, :],
                                     start=False, stop=(h == HG - 1), skip_group_check=True)
                last.then_inc(l_ready, 1)

            def scan_outputs(c, j, s):
                t, gg = s // 2, s % 2
                n = c * 4 * AJ + j * 4 + s
                pe.wait_ge(m_done, n + 3)
                pe.wait_ge(y_free, n + 1)
                if s >= 2:
                    pe.wait_ge(st_used, n - 1 + STATE)
                pe.matmul(ybank[:, GW:2 * GW], CT[:, gg, t * P:(t + 1) * P],
                          state[:, ds(j * 2 * GW + gg * GW, GW)], start=True, stop=True)
                for h in range(HG):
                    last = pe.matmul(ybank[:, h * HD:(h + 1) * HD], mm[:, s % 2, h, :],
                                     xd[:, s % 2, h * HD:(h + 1) * HD], start=True, stop=True)
                last.then_inc(y_ready, 1)
                pe.wait_ge(st_used, n + STATE)
                pe.matmul(stbank[:, 0:GW], btok[:, t, gg * P:(gg + 1) * P], xdd[:, s % 2, :],
                          start=True, stop=True).then_inc(st_ready, 1)

            def front(c):
                pe.wait_ge(xt_ready, (c + 1) * 16)
                dt_stage(c)
                with pe.Fori(0, AJ) as j:
                    for n in range(8):
                        w = block_in(c, j * (8 // RING), n)
                        dst_ = bank(c, j * MA, n)
                        last = (tokens if n in (4, 5) else channels)(dst_, w, xT)
                        last.then_inc(block_done, 1)
                    conv0 = c * 4 * AJ + j * 4 + CONV
                    pe.wait_ge(conv_act, conv0 + 2)
                    for t in range(NT):
                        dst_ = turn_bank(c, j * TA, t)
                        for ct in range(4):
                            last = pe.transpose(dst_[:, ct * P:(ct + 1) * P], xs[:, ct, t * P:(t + 1) * P], ident[:, :])
                        last.then_inc(turn_ready, 1)
                    pe.wait_ge(conv_act, conv0 + 4)
                    dst_ = turn_bank(c, j * TA, 2)
                    for t in range(NT):
                        for ct in range(2):
                            last = pe.transpose(dst_[:, t * 256 + ct * P:t * 256 + (ct + 1) * P],
                                                BT[:, ct, t * P:(t + 1) * P], ident[:, :])
                    last.then_inc(turn_ready, 1)
                    pe.wait_ge(pw_ready, (c * AJ + j + 1) * 16)
                    pe.wait_ge(pool_done, c * AJ + j + 1)
                    dst_ = turn_bank(c, j * TA, 3)
                    for ct in range(2):
                        for k in range(2):
                            last = pe.matmul(dst_[:, ct * T:(ct + 1) * T], pw[:, k, ct * P:(ct + 1) * P],
                                             pooled[:, k, :], start=(k == 0), stop=(k == 1))
                    last.then_inc(turn_ready, 1)
                    pe.wait_ge(adtc_ready, c * AJ + j + 1)
                    unturned(pe, c, j * TA + 3)
                    scan_scores(c, j, 0)
                    for s in range(4):
                        if s < 3:
                            scan_scores(c, j, s + 1)
                        scan_outputs(c, j, s)
                    pe.wait_ge(yn_ready, c * AJ + j + 1)
                    for gg in range(2):
                        dst_ = turn_bank(c, j * TA, 4 + gg)
                        for ct in range(2):
                            for t in range(NT):
                                last = pe.transpose(dst_[:, ct * T + t * P:ct * T + (t + 1) * P],
                                                    yg[:, t, gg * GW + ct * P:gg * GW + (ct + 1) * P], ident[:, :])
                        last.then_inc(turn_ready, 1)
                unturned(pe, c, AJ * TA)
                for q in range(4):
                    w = block_in(c, BA // RING, 3 * q)
                    dst_ = bank(c, AJ * MA, 2 * q)
                    channels(dst_, w, xT).then_inc(block_done, 1)
                    lo, hi = block_in(c, BA // RING, 3 * q + 1), block_in(c, BA // RING, 3 * q + 2)
                    dst_ = bank(c, AJ * MA, 2 * q + 1)
                    for ct in range(2):
                        for k in range(2 * KD):
                            last = pe.matmul(dst_[:, ct * T:(ct + 1) * T], (lo, hi)[k // KD][:, k % KD, ct * P:(ct + 1) * P],
                                             yT[:, k, :], start=(k == 0), stop=(k == 2 * KD - 1))
                    last.then_inc(block_done, 2)
                pe.wait_ge(pair_merged, (c + 1) * 4)
                for n in range(4):
                    w = block_in(c, (BA + BC) // RING, n)
                    dst_ = bank(c, AJ * MA + MC, n)
                    tokens(dst_, w, merged).then_inc(block_done, 1)
                pe.wait_ge(h_ready, c + 1)
                for n in range(4):
                    dst_ = turn_bank(c, AJ * TA, n)
                    for ct in range(2):
                        for t in range(NT):
                            last = pe.transpose(dst_[:, ct * T + t * P:ct * T + (t + 1) * P],
                                                hf[:, t, (2 * n + ct) * P:(2 * n + ct + 1) * P], ident[:, :])
                    last.then_inc(turn_ready, 1)
                with pe.Fori(0, 2) as i:
                    def query(hh):
                        w = block_in(c, (BA + BC + BW) // RING + i, hh)
                        dst_ = bank(c, AJ * MA + MC + MW + i * 4, hh)
                        channels(dst_, w, hT).then_inc(block_done, 1)

                    def score(hh):
                        emptied(pe, c, AJ * MA + MC + MW + i * 4 + hh + 1)
                        dst_ = turn_bank(c, AJ * TA + TW + i * 4, hh)
                        for t in range(NT):
                            for side in range(2):
                                n = t * 2 + side
                                last = pe.matmul(dst_[:, n * KEYS:(n + 1) * KEYS], qT[:, hh % 2, side, t * P:(t + 1) * P],
                                                 subk[:, side, :], start=True, stop=True)
                        last.then_inc(turn_ready, 1)

                    unturned(pe, c, AJ * TA + TW)
                    query(0)
                    for hh in range(4):
                        if hh < 3:
                            query(hh + 1)
                        score(hh)

            pe.sem_inc(block_done, RING)
            pe.sem_inc(turn_ready, TURNED)
            pe.wait_ge(const_dma, 16 * NCONST)
            pe.wait_ge(const_made, 11)
            pe.wait_ge(dve_ready, 1)
            with pe.Fori(0, NC) as c:
                front(c)

        @block.scalar
        def _(act):
            def filled(c, blocks, m):
                act.wait_ge(block_done, c * BLOCKS + blocks + RING)
                return main[m % 2]

            def turned(c, m, n):
                act.wait_ge(turn_ready, c * TURNS + m + n + 1 + TURNED)
                return turn[n % 2]

            def silu_conv(c, j, n):
                act.wait_ge(conv_out, c * 4 * AJ + j * 4 + n + 1 + CONV)
                dst_ = (xs[:, 0:2, :], xs[:, 2:4, :], BT[:, :, :], CT[:, :, :])[n]
                act.activation(dst_, cout[:, n % 2, :, :], ACT.Silu).then_inc(conv_act, 1)

            def raw_conv(c, j, n):
                src = filled(c, j * 8 + n + 1, n)[:, :].rearrange("p (a t) -> p a t", a=2)
                act.wait_ge(conv_out, c * 4 * AJ + j * 4 + n + 1)
                tail = ctail[:, ds(j * 8 + n * 2, 2), :]
                act.copy(craw[:, n % 2, :, 3:3 + T], src).then_inc(main_free, 1)
                act.copy(craw[:, n % 2, :, 0:3], tail)
                act.drain()
                act.copy(tail, craw[:, n % 2, :, T:T + 3]).then_inc(conv_raw, 1)

            def front_dt(c):
                act.wait_ge(dt_abs, c + 1)
                act.activation(dte[:, :], dte[:, :], ACT.Exp).then_inc(dt_exp, 1)
                act.wait_ge(dt_u, c + 1)
                act.activation(dtl[:, :], dtu[:, :], ACT.Ln).then_inc(dt_ln, 1)
                act.wait_ge(dec_in, c + 1)
                act.activation(dst[:, :], dst[:, :], ACT.Exp)
                act.activation(eacum[:, :], stbank[:, 320:320 + NTH], ACT.Exp)
                act.activation(cdec[:, :], stbank[:, 384:384 + NTH], ACT.Exp).then_inc(dec_ready, 1)

            def front_a1(c, j):
                raw_conv(c, j, 0)
                raw_conv(c, j, 1)
                silu_conv(c, j, 0)
                raw_conv(c, j, 2)
                silu_conv(c, j, 1)
                raw_conv(c, j, 3)

            def front_a2(c, j):
                silu_conv(c, j, 2)
                silu_conv(c, j, 3)
                for n in (4, 5):
                    src = filled(c, j * 8 + n + 1, n)[:, :].rearrange("p (t n) -> p t n", t=NT)
                    last = act.activation(zs[:, :, (n - 4) * 256:(n - 3) * 256], src, ACT.Silu)
                    last.then_inc(main_free, 1)
                src = filled(c, j * 8 + 7, 6)[:, :].rearrange("p (a t) -> p a t", a=2)
                tail = ptail[:, ds(j * 2, 2), :]
                act.copy(praw[:, :, HALO:], src).then_inc(main_free, 1)
                act.copy(praw[:, :, 0:HALO], tail)
                act.drain()
                act.copy(tail, praw[:, :, T:T + HALO]).then_inc(pool_raw, 1)

            def front_a3(c, j):
                src = filled(c, j * 8 + 8, 7)[:, :].rearrange("p (a t) -> p a t", a=2)
                act.activation(gps, src, ACT.Sigmoid).then_inc(main_free, 1)
                for t in range(NT):
                    act.copy(xtok[:, t, :], turned(c, j * TA, t)[:, :]).then_inc(turn_free, 1)
                act.copy(btok[:, :, :], turned(c, j * TA, 2)[:, :].rearrange("p (t n) -> p t n", t=NT)
                         ).then_inc(turn_free, 1)
                src = turned(c, j * TA, 3)
                for ct in range(2):
                    last = act.activation(asb[:, ct, :], src[:, ct * T:(ct + 1) * T], ACT.Copy,
                                          scale=psc[:, ds(j * 2 + ct, 1)])
                last.then_inc(turn_free, 1)

            def decays(c, j, s):
                n = c * 4 * AJ + j * 4 + s
                act.wait_ge(l_ready, n + 1)
                act.wait_ge(m_done, n + 1)
                t, gg = s // 2, s % 2
                for h in range(HG):
                    last = act.activation(lexp[:, s % 2, h, :], lbank[:, h * P:(h + 1) * P], ACT.Exp,
                                          bias=nacum[:, ds(t * HEADS + j * 2 * HG + gg * HG + h, 1)])
                last.then_inc(lexp_ready, 1)

            def front_a4(c, j):
                for s in range(4):
                    decays(c, j, s)
                act.wait_ge(rms_in, c * AJ + j + 1)
                act.activation(rms[:, :], rms[:, :], ACT.Sqrt).then_inc(rms_sqrt, 1)
                act.wait_ge(rms_rstd, c * AJ + j + 1)
                for s in range(4):
                    y = yg[:, s // 2, (s % 2) * GW:(s % 2 + 1) * GW]
                    last = act.activation(y, y, ACT.Copy, scale=rmsr[:, s:s + 1])
                last.then_inc(yn_ready, 1)
                for gg in range(2):
                    src = turned(c, j * TA, 4 + gg)
                    for ct in range(2):
                        k = j * 4 + gg * 2 + ct
                        last = act.activation(yT[:, ds(k, 1), :], src[:, ct * T:(ct + 1) * T].unsqueeze(1), ACT.Copy,
                                              scale=nw[:, ds(k, 1)])
                    last.then_inc(turn_free, 1)

            def front_pair(c, q):
                if q >= 2:
                    act.wait_ge(pair_merged, c * 4 + q - 1)
                flat = lexp[:, q % 2, :, :].rearrange("p a b -> p (a b)")
                act.activation(flat, filled(c, BA + 3 * q + 1, 0)[:, :], ACT.Sigmoid).then_inc(main_free, 1)
                flat = mm[:, q % 2, :, :].rearrange("p a b -> p (a b)")
                act.copy(flat, filled(c, BA + 3 * q + 3, 1)[:, :]).then_inc(main_free, 1)

            def front_w(c):
                for n in range(4):
                    src = filled(c, BA + BC + n + 1, n)[:, :].rearrange("p (t n) -> p t n", t=NT)
                    act.copy(hf[:, :, n * 256:(n + 1) * 256], src).then_inc(main_free, 1)
                act.wait_ge(ln1_var, c + 1)
                act.activation(lstd[:, :], lstd[:, :], ACT.Sqrt).then_inc(ln1_std, 1)
                for n in range(4):
                    src = turned(c, AJ * TA, n)[:, :].rearrange("p (a t) -> p a t", a=2)
                    act.copy(hT[:, 2 * n:2 * n + 2, :], src).then_inc(turn_free, 1)

            def front_d(c, i, half):
                def query(hh):
                    src = filled(c, BA + BC + BW + i * 4 + hh + 1, hh)[:, :].rearrange("p (a t) -> p a t", a=2)
                    act.copy(qT[:, hh % 2, :, :], src).then_inc(main_free, 1)

                def score(hh):
                    src = turned(c, AJ * TA + TW + i * 4, hh)[:, :].rearrange("p (a n) -> p a n", a=4)
                    act.wait_ge(topk_done, c * PH + i * 4 + hh + 1)
                    act.copy(ssb[:, hh % 2, :, :], src).then_inc(turn_free, 1)

                if half == 0:
                    query(0)
                    query(1)
                    score(0)
                    query(2)
                    score(1)
                elif half == 1:
                    query(3)
                    score(2)
                    score(3)
                elif half == 3:
                    act.wait_ge(sm_in, c * 2 + i + 1)
                    act.activation(bex, bex, ACT.Exp).then_inc(sm_exp, 1)

            def gelu(c, u, b):
                act.wait_ge(row_free, (c * UNITS + u) * 2 * TOPK + TOPK + ROWS)
                act.activation(hgel[:, b, :], hdot[:, b, :], ACT.Gelu).then_inc(gelu_ready, 1)

            def finish_tile(c, t):
                act.wait_ge(ln2_var, c * NT + t + 1)
                act.activation(pstd[:, :], pstd[:, :], ACT.Sqrt).then_inc(ln2_std, 1)
                act.wait_ge(out_ready, c * NT + t + 1)
                act.dma_start(out[ds(c * T + t * P, P), :], acc[:, :]).then_inc(out_done, 16)

            def superchunk(cf, cp):
                if cf is not None:
                    front_dt(cf)
                with act.Fori(0, AJ) as j:
                    if cf is not None:
                        front_a1(cf, j)
                    if cp is not None:
                        gelu(cp, j * 2, 0)
                    if cf is not None:
                        front_a2(cf, j)
                        front_a3(cf, j)
                    if cp is not None:
                        gelu(cp, j * 2 + 1, 1)
                    if cf is not None:
                        front_a4(cf, j)
                if cp is not None:
                    finish_tile(cp, 0)
                for i in range(2):
                    if cf is not None:
                        front_pair(cf, 2 * i)
                    if cp is not None:
                        gelu(cp, 8 + i, i)
                    if cf is not None:
                        front_pair(cf, 2 * i + 1)
                if cf is not None:
                    front_w(cf)
                if cp is not None:
                    gelu(cp, 10, 0)
                    gelu(cp, 11, 1)
                with act.Fori(0, 2) as i:
                    for b in range(2):
                        if cf is not None:
                            front_d(cf, i, 2 * b)
                        if cp is not None:
                            gelu(cp, 12 + i * 2 + b, b)
                        if cf is not None:
                            front_d(cf, i, 2 * b + 1)
                if cp is not None:
                    finish_tile(cp, 1)

            act.dma_start(lnb2[:, :], ln2b.to_broadcast([P, D])).then_inc(out_done, 16)
            act.sem_inc(main_free, BANKS)
            act.sem_inc(turn_free, BANKS)
            act.sem_inc(lexp_ready, LEXP)
            act.sem_inc(conv_act, CONV)
            act.wait_ge(const_dma, 16 * NCONST)
            act.activation(a_s[:, :], a_s[:, :], ACT.Exp).then_inc(a_made, 1)
            act.wait_ge(dve_ready, 1)
            superchunk(0, None)
            with act.Fori(0, NC - 1) as c:
                superchunk(c + 1, c)
            superchunk(None, NC - 1)
            act.wait_ge(out_done, 16 * (NC * NT + 1))

        @block.vector
        def _(dve):
            def front_dt(c):
                dve.wait_ge(dt_proj, c + 1)
                dve.tensor_tensor(dtv[:, :].rearrange("p (t h) -> p t h", t=NT),
                                  stbank[:, 256:256 + NTH].rearrange("p (t h) -> p t h", t=NT),
                                  dtb_s[:, :].unsqueeze(1).to_broadcast([P, NT, HEADS]), ALU.add)
                dve.drain()
                dve.tensor_scalar(dtu[:, :], dtv[:, :], -1.0, None, ALU.mult)
                dve.drain()
                dve.tensor_tensor(dte[:, :], dtv[:, :], dtu[:, :], ALU.min).then_inc(dt_abs, 1)
                dve.wait_ge(dt_exp, c + 1)
                dve.tensor_scalar(dtu[:, :], dte[:, :], 1.0, None, ALU.add).then_inc(dt_u, 1)
                dve.drain()
                dve.tensor_scalar(dt_[:, :], dtu[:, :], -1.0, None, ALU.add)
                dve.reciprocal(adt[:, :], dtu[:, :])
                dve.drain()
                dve.tensor_tensor(dte[:, :], dte[:, :], dt_[:, :], ALU.subtract)
                dve.drain()
                dve.tensor_tensor(dte[:, :], dte[:, :], adt[:, :], ALU.mult)
                dve.drain()
                dve.wait_ge(dt_ln, c + 1)
                dve.tensor_tensor(dtl[:, :], dtl[:, :], dte[:, :], ALU.add)
                dve.drain()
                dve.scalar_tensor_tensor(out=dt_[:, :], in0=dtv[:, :], scalar=0.0, in1=dtl[:, :],
                                         op0=ALU.max, op1=ALU.add)
                dve.drain()
                dve.tensor_tensor(adt[:, :].rearrange("p (t h) -> p t h", t=NT),
                                  dt_[:, :].rearrange("p (t h) -> p t h", t=NT),
                                  a_s[:, :].unsqueeze(1).to_broadcast([P, NT, HEADS]), ALU.mult).then_inc(adt_ready, 1)
                dve.wait_ge(acum_ready, c + 1)
                dve.tensor_scalar(nacum[:, :], stbank[:, 320:320 + NTH], -1.0, None, ALU.mult)
                dve.drain()
                dve.tensor_tensor(dst[:, :], stbank[:, 384:384 + NTH], nacum[:, :], ALU.add).then_inc(dec_in, 1)
                dve.wait_ge(dec_ready, c + 1)
                dve.tensor_tensor(dst[:, :], dst[:, :], dt_[:, :], ALU.mult)
                dve.drain()

            def conv(c, j, n):
                k0 = c * 4 * AJ + j * 4 + n
                dve.wait_ge(conv_raw, k0 + 1)
                dve.wait_ge(conv_act, k0 + 1)
                for k in range(TAPS):
                    for ct in range(2):
                        col = j * 8 + n * 2 + ct
                        src, o = craw[:, n % 2, ct, k:k + T], cout[:, n % 2, ct, :]
                        wk = cw[:, ds(col, 1), k:k + 1].rearrange("p a b -> p (a b)")
                        if k == 0:
                            last = dve.tensor_scalar(o, src, wk, cbias[:, ds(col, 1)], ALU.mult, ALU.add)
                        else:
                            last = dve.scalar_tensor_tensor(out=o, in0=src, scalar=wk, in1=o, op0=ALU.mult, op1=ALU.add)
                    if k < TAPS - 1:
                        dve.drain()
                        yield
                last.then_inc(conv_out, 1)
                yield

            def pooling(c, j, first):
                dve.wait_ge(pool_raw, c * AJ + j + 1)
                E = HALO + T
                src, dst_, reach = praw, psa, 1
                for w in range(4):
                    lo = 2 * reach - 1
                    dve.tensor_tensor(dst_[:, :, lo:E], src[:, :, lo:E], src[:, :, lo - reach:E - reach], ALU.add)
                    dve.drain()
                    fixed = dst_[:, :, HALO:E]
                    if first:
                        fixed = yt1[:, 0:32].rearrange("p (a t) -> p a t", a=2)
                        dve.tensor_tensor(fixed, dst_[:, :, HALO:HALO + 16],
                                          pfix[:, w, :].unsqueeze(1).to_broadcast([P, 2, 16]), ALU.mult)
                        dve.drain()
                        spans = ((fixed, slice(0, 16)), (dst_[:, :, HALO + 16:E], slice(16, T)))
                    else:
                        spans = ((fixed, slice(0, T)),)
                    coef = pcoef[:, ds(j, 1), w:w + 1].rearrange("p a b -> p (a b)")
                    for s, to in spans:
                        o = pooled[:, :, to]
                        if w == 0:
                            raw = praw[:, :, HALO + to.start:HALO + to.stop]
                            last = dve.scalar_tensor_tensor(out=o, in0=s, scalar=coef, in1=raw,
                                                            op0=ALU.mult, op1=ALU.subtract)
                        else:
                            last = dve.scalar_tensor_tensor(out=o, in0=s, scalar=coef, in1=o,
                                                            op0=ALU.mult, op1=ALU.add)
                    if w == 3:
                        last.then_inc(pool_done, 1)
                    dve.drain()
                    src, dst_, reach = dst_, (psb if dst_ is psa else psa), 2 * reach
                    yield

            def merge_pool(c, j):
                unturned(dve, c, j * TA + 4)
                dve.tensor_tensor(merged[:, ds(j * 2, 2), :], asb, gps, ALU.mult)
                yield

            def scan_pre(c, j, s):
                t, gg = s // 2, s % 2
                n = c * 4 * AJ + j * 4 + s
                xv = xtok[:, t, gg * GW:(gg + 1) * GW].rearrange("p (h d) -> p h d", h=HG)
                dve.tensor_tensor(xd[:, s % 2, :].rearrange("p (h d) -> p h d", h=HG), xv,
                                  spread(heads(dt_, t, j, gg), HD), ALU.mult)
                dve.tensor_tensor(xdd[:, s % 2, :].rearrange("p (h d) -> p h d", h=HG), xv,
                                  spread(heads(dst, t, j, gg), HD), ALU.mult)
                yield
                dve.wait_ge(cb_ready, n + 1)
                dve.wait_ge(lexp_ready, n + 1 + LEXP)
                dve.tensor_tensor(mm[:, s % 2, :, :], lexp[:, s % 2, :, :],
                                  cbbank[:, 0:P].unsqueeze(1).to_broadcast([P, HG, P]), ALU.mult).then_inc(m_done, 1)
                yield

            def scan_post(c, j, s):
                t, gg = s // 2, s % 2
                n = c * 4 * AJ + j * 4 + s
                xv = xtok[:, t, gg * GW:(gg + 1) * GW].rearrange("p (h d) -> p h d", h=HG)
                y3 = yt1[:, :].rearrange("p (h d) -> p h d", h=HG)
                dve.drain()
                dve.tensor_tensor(yt2[:, :].rearrange("p (h d) -> p h d", h=HG), xv,
                                  spread(dsk[:, ds(j * 2 * HG + gg * HG, HG)], HD), ALU.mult)
                st = state[:, ds(j * 2 * GW + gg * GW, GW)]
                dve.wait_ge(y_ready, n + 1)
                dve.tensor_tensor(y3, ybank[:, GW:2 * GW].rearrange("p (h d) -> p h d", h=HG),
                                  spread(heads(eacum, t, j, gg), HD), ALU.mult)
                dve.tensor_tensor(st.rearrange("p (h d) -> p h d", h=HG), st.rearrange("p (h d) -> p h d", h=HG),
                                  spread(heads(cdec, t, j, gg), HD), ALU.mult)
                dve.drain()
                dve.tensor_tensor(yt1[:, :], yt1[:, :], ybank[:, 0:GW], ALU.add).then_inc(y_free, 1)
                dve.wait_ge(st_ready, n + 1)
                dve.tensor_tensor(st, st, stbank[:, 0:GW], ALU.add).then_inc(st_used, 1)
                yield
                dve.drain()
                dve.tensor_tensor(yt1[:, :], yt1[:, :], yt2[:, :], ALU.add)
                dve.drain()
                y = yg[:, t, gg * GW:(gg + 1) * GW]
                dve.tensor_tensor(y, yt1[:, :], zs[:, t, gg * GW:(gg + 1) * GW], ALU.mult)
                dve.drain()
                dve.tensor_tensor_reduce(yt2[:, :], y, y, 1.0, 0.0, ALU.mult, ALU.add, rms[:, s:s + 1])
                yield

            def rms_scale(c, j):
                dve.drain()
                dve.tensor_scalar(rms[:, :], rms[:, :], 1.0 / GW, EPS, ALU.mult, ALU.add).then_inc(rms_in, 1)
                yield
                dve.wait_ge(rms_sqrt, c * AJ + j + 1)
                dve.reciprocal(rmsr[:, :], rms[:, :]).then_inc(rms_rstd, 1)
                yield

            def front_a1(c, j):
                yield from conv(c, j, 0)
                yield from conv(c, j, 1)

            def front_a2(c, j, first):
                yield from conv(c, j, 2)
                yield from conv(c, j, 3)
                yield from pooling(c, j, first)

            def front_a3(c, j):
                yield from merge_pool(c, j)
                for t in range(NT):
                    last = dve.tensor_copy(adtc[:, t, :], adt[:, ds(t * HEADS + j * 2 * HG, 2 * HG)])
                last.then_inc(adtc_ready, 1)
                unturned(dve, c, j * TA + 3)
                emptied(dve, c, j * MA + 6)

            def front_a4(c, j):
                yield from scan_pre(c, j, 0)
                for s in range(4):
                    if s < 3:
                        yield from scan_pre(c, j, s + 1)
                    yield from scan_post(c, j, s)
                yield from rms_scale(c, j)

            def front_pair(c, q):
                g = lexp[:, q % 2, :, :].rearrange("p a b -> p (a b)")
                m = mm[:, q % 2, :, :].rearrange("p a b -> p (a b)")
                dst_ = mflat[:, q * 512:(q + 1) * 512]
                emptied(dve, c, AJ * MA + 2 * q + 2)
                dve.tensor_tensor(m, m, g, ALU.mult)
                dve.drain()
                dve.tensor_tensor(dst_, dst_, m, ALU.add).then_inc(pair_merged, 1)
                yield

            def front_w(c):
                emptied(dve, c, AJ * MA + MC + MW)
                dve.wait_ge(xres_ready, (c + 1) * 16)
                for t in range(NT):
                    h = hf[:, t, :]
                    dve.scalar_tensor_tensor(out=h, in0=xres[:, t, :], scalar=ALPHA, in1=h, op0=ALU.mult, op1=ALU.add)
                    dve.drain()
                    yield
                    for a in range(2):
                        dve.bn_stats(stats[:, t, a, :], hf[:, t, a * 512:(a + 1) * 512])
                    dve.drain()
                    dve.bn_aggr(mv[:, t, :], stats[:, t, :, :])
                    yield
                dve.drain()
                dve.tensor_scalar(lstd[:, :], mv[:, :, 1], EPS, None, ALU.add).then_inc(ln1_var, 1)
                dve.wait_ge(ln1_std, c + 1)
                dve.reciprocal(lrst[:, :], lstd[:, :])
                for t in range(NT):
                    h = hf[:, t, :]
                    dve.drain()
                    dve.tensor_scalar(h, h, mv[:, t, 0:1], lrst[:, t:t + 1], ALU.subtract, ALU.mult)
                    dve.drain()
                    yield
                    dve.tensor_tensor(h, h, lng1[:, :], ALU.mult)
                    dve.drain()
                    yield
                    last = dve.tensor_tensor(h, h, lnb1[:, :], ALU.add)
                    yield
                last.then_inc(h_ready, 1)
                dve.drain()

            def side_topk(c, i, hh):
                unturned(dve, c, AJ * TA + TW + i * 4 + hh + 1)
                dve.memset(bsum, 0.0)
                for t in range(NT):
                    for side in range(2):
                        u = hh * 2 + t
                        s = ssb[:, hh % 2, t * 2 + side, :]
                        dve.max(tm[:, u, side, 0:8], s)
                        dve.drain()
                        dve.max_index(tmi[:, u, side, 0:8], tm[:, u, side, 0:8], s)
                        dve.match_replace(snext, tm[:, u, side, 0:8], s, LOWEST)
                        dve.drain()
                        dve.max(tm[:, u, side, 8:16], snext)
                        dve.drain()
                        last = dve.max_index(tmi[:, u, side, 8:16], tm[:, u, side, 8:16], snext)
                        yield
                last.then_inc(topk_done, 1)

            def candidates():
                dve.drain()
                dve.tensor_copy(tf, tmi[:, :, :, :])
                dve.drain()
                dve.tensor_scalar(tf[:, :, 0, :], tf[:, :, 0, :], float(KEYS), None, ALU.mult)
                dve.drain()
                for src, dst_ in ((tm, cand), (tf, candi)):
                    at = 0
                    for a in range(5):
                        n = TOPK // (a + 1)
                        dve.tensor_tensor(dst_[:, :, at:at + n], src[:, :, 1, 0:n],
                                          src[:, :, 0, a:a + 1].to_broadcast([P, 8, n]), ALU.add)
                        at += n
                    for a in range(5, 8):
                        dve.tensor_tensor(dst_[:, :, at:at + 2], src[:, :, 1, 0:2],
                                          src[:, :, 0, a:a + 1].to_broadcast([P, 8, 2]), ALU.add)
                        at += 2
                    dve.tensor_tensor(dst_[:, :, at:at + 8], src[:, :, 0, 8:16],
                                      src[:, :, 1, 0:1].to_broadcast([P, 8, 8]), ALU.add)
                    yield
                dve.drain()
                for u in range(8):
                    s = cand[:, u, :]
                    dve.max(bm[:, u, 0:8], s)
                    dve.drain()
                    dve.max_index(pos[:, u, 0:8], bm[:, u, 0:8], s)
                    dve.match_replace(cnext, bm[:, u, 0:8], s, LOWEST)
                    dve.drain()
                    dve.max(bm[:, u, 8:16], cnext)
                    dve.drain()
                    dve.max_index(pos[:, u, 8:16], bm[:, u, 8:16], cnext)
                    if u % 2:
                        yield
                dve.drain()
                dve.tensor_copy(posf, pos[:, :, :])
                dve.tensor_tensor(bex, bm, bm[:, :, 0:1].to_broadcast([P, 8, TOPK]), ALU.subtract).then_inc(sm_in, 1)
                dve.drain()
                yield

            def choose(c, i):
                for u in range(8):
                    dve.tensor_tensor(sel1, iota[:, :].unsqueeze(1).to_broadcast([P, TOPK, NCAND]),
                                      spread(posf[:, u, :], NCAND), ALU.is_equal)
                    dve.drain()
                    dve.tensor_tensor(sel1, sel1, candi[:, u, :].unsqueeze(1).to_broadcast([P, TOPK, NCAND]), ALU.mult)
                    dve.drain()
                    yield
                    dve.tensor_reduce(self_[:, u, :], sel1, AX.X, ALU.add)
                    dve.drain()
                    yield
                dve.wait_ge(sm_exp, c * 2 + i + 1)
                dve.tensor_reduce(bsum, bex, AX.X, ALU.add)
                dve.drain()
                dve.reciprocal(bsum, bsum)
                dve.drain()
                for t in range(NT):
                    to = ds(t * PH + i * 4, 4)
                    dve.tensor_copy(idxf[:, to, :], self_[:, t:8:2, :])
                    dve.tensor_tensor(gatef[:, to, :], bex[:, t:8:2, :],
                                      spread(bsum.rearrange("p (h t) -> p h t", t=NT)[:, :, t], TOPK), ALU.mult)
                dve.drain()
                yield

            def front_d(c, i, quarter):
                if quarter < 2:
                    yield from side_topk(c, i, 2 * quarter)
                    yield from side_topk(c, i, 2 * quarter + 1)
                elif quarter == 2:
                    yield from candidates()
                else:
                    yield from choose(c, i)

            def take_over():
                dve.tensor_copy(idxp[:, 0:UNITS, :], idxf[:, :, :])
                dve.tensor_copy(gatep[:, :, :], gatef[:, :, :])
                dve.tensor_copy(hp[:, :, :], hf[:, :, :])
                dve.drain()

            def next_indices(u, b):
                dve.tensor_copy(icur[b][:, :].unsqueeze(1), idxp[:, ds(u, 1), :]).then_inc(idx_ready, 1)

            def dots(c, t, u, b):
                for k in range(TOPK):
                    dve.wait_ge(row_ready[k % ROWS], (c * UNITS * 4 + u * 4 + k // ROWS + 1) * 16)
                    r = rows[k % ROWS][:, :]
                    last = dve.tensor_tensor_reduce(r, r, hp[:, t, :], 1.0, 0.0, ALU.mult, ALU.add, hdot[:, b, k:k + 1])
                    last.then_inc(row_free, 1)
                    yield

            def sums(c, u, b):
                dve.wait_ge(gelu_ready, c * UNITS + u + 1)
                dve.tensor_tensor(hact[:, b:b + 1, :], hgel[:, b:b + 1, :], gatep[:, ds(u, 1), :], ALU.mult)
                for k in range(TOPK):
                    dve.drain()
                    dve.wait_ge(row_ready[k % ROWS], (c * UNITS * 4 + u * 4 + 2 + k // ROWS + 1) * 16)
                    dve.scalar_tensor_tensor(out=acc[:, :], in0=rows[k % ROWS][:, :], scalar=hact[:, b, k:k + 1],
                                             in1=acc[:, :], op0=ALU.mult, op1=ALU.add).then_inc(row_free, 1)
                    yield

            def start_tile(c, t):
                dve.wait_ge(out_done, (c * NT + t + 1) * 16)
                dve.tensor_scalar(acc[:, :], hp[:, t, :], ALPHA, None, ALU.mult)

            def finish_tile(c, t):
                dve.drain()
                for a in range(2):
                    dve.bn_stats(pstats[:, a, :], acc[:, a * 512:(a + 1) * 512])
                dve.drain()
                dve.bn_aggr(pmv[:, :], pstats[:, :, :])
                dve.drain()
                dve.tensor_scalar(pstd[:, :], pmv[:, 1:2], EPS, None, ALU.add).then_inc(ln2_var, 1)
                dve.wait_ge(ln2_std, c * NT + t + 1)
                dve.reciprocal(prst[:, :], pstd[:, :])
                dve.drain()
                dve.tensor_scalar(acc[:, :], acc[:, :], pmv[:, 0:1], prst[:, :], ALU.subtract, ALU.mult)
                dve.drain()
                dve.tensor_tensor(acc[:, :], acc[:, :], lng2[:, :], ALU.mult)
                dve.drain()
                dve.tensor_tensor(acc[:, :], acc[:, :], lnb2[:, :], ALU.add).then_inc(out_ready, 1)

            def none():
                return iter(())

            def superchunk(cf, cp, first=False):
                f, e = cf is not None, cp is not None
                if e:
                    take_over()
                if f:
                    front_dt(cf)
                if e:
                    start_tile(cp, 0)
                with dve.Fori(0, AJ) as j:
                    for b in range(2):
                        a, z = ((front_a1(cf, j), front_a2(cf, j, first)) if b == 0
                                else (front_a3(cf, j), front_a4(cf, j))) if f else (none(), none())
                        if e:
                            next_indices(j * 2 + b + 1, 1 - b)
                        weave(dots(cp, 0, j * 2 + b, b) if e else none(), a)
                        weave(sums(cp, j * 2 + b, b) if e else none(), z, 2 if b else 1)
                if e:
                    finish_tile(cp, 0)
                for i in range(2):
                    if e:
                        next_indices(9 + i, 1 - i)
                    weave(dots(cp, 1, 8 + i, i) if e else none(), front_pair(cf, 2 * i) if f else none())
                    if e and i == 0:
                        start_tile(cp, 1)
                    weave(sums(cp, 8 + i, i) if e else none(), front_pair(cf, 2 * i + 1) if f else none())
                if e:
                    next_indices(11, 1)
                weave(dots(cp, 1, 10, 0) if e else none(), front_w(cf) if f else none())
                if e:
                    weave(sums(cp, 10, 0), none())
                    next_indices(12, 0)
                    weave(dots(cp, 1, 11, 1), none())
                    weave(sums(cp, 11, 1), none())
                with dve.Fori(0, 2) as i:
                    if e:
                        dve.tensor_copy(idxp[:, UNITS, :], idxf[:, 0, :])
                        dve.drain()
                    for b in range(2):
                        if e:
                            next_indices(13 + i * 2 + b, 1 - b)
                        weave(dots(cp, 1, 12 + i * 2 + b, b) if e else none(), front_d(cf, i, 2 * b) if f else none())
                        weave(sums(cp, 12 + i * 2 + b, b) if e else none(), front_d(cf, i, 2 * b + 1) if f else none())
                if e:
                    finish_tile(cp, 1)

            dve.sem_inc(conv_out, CONV)
            dve.sem_inc(m_done, 2)
            dve.sem_inc(y_free, 1)
            dve.sem_inc(st_used, STATE)
            dve.sem_inc(topk_done, 2)
            dve.sem_inc(row_free, ROWS)
            dve.memset(pcoef[:, :, :], 0.0)
            dve.memset(ctail[:, :, :], 0.0)
            dve.memset(ptail[:, :, :], 0.0)
            dve.memset(state[:, :], 0.0)
            dve.drain()
            for w in range(4):
                dve.memset(pcoef[:, w, w:w + 1], 1.0 / WINDOWS[w])
            dve.wait_ge(const_made, 11)
            for w in range(4):
                dve.tensor_scalar(pfix[:, w, :], pfix[:, w, :], float(WINDOWS[w]), None, ALU.min)
            dve.drain()
            dve.reciprocal(pfix[:, :, :], pfix[:, :, :])
            dve.drain()
            for w in range(4):
                dve.tensor_scalar(pfix[:, w, :], pfix[:, w, :], float(WINDOWS[w]), None, ALU.mult)
            dve.wait_ge(const_dma, 16 * NCONST)
            dve.wait_ge(a_made, 1)
            dve.tensor_scalar(a_s[:, :], a_s[:, :], -1.0, None, ALU.mult).then_inc(dve_ready, 1)
            dve.drain()
            superchunk(0, None, first=True)
            dve.tensor_copy(icur[0][:, :], idxf[:, 0, :]).then_inc(idx_ready, 1)
            with dve.Fori(0, NC - 1) as c:
                superchunk(c + 1, c)
            superchunk(None, NC - 1)


_OUT = (1, SEQ, D)


def kernel(**inputs):
    import numpy as np
    import concourse.bacc as bacc
    from concourse.bass_utils import run_bass_kernel_spmd

    a = {k: np.asarray(v) for k, v in inputs.items()}
    w_in = a["w_in"][0]
    at = {"pool": 0, "z": D, "x": D + INNER, "B": D + 2 * INNER, "C": D + 2 * INNER + D,
          "dt": 2 * D + INNER * 2 + D, "gp": 2 * D + INNER * 2 + D + HEADS, "gs": 3 * D + INNER * 2 + D + HEADS}

    def blk(w, col):
        return w[:, col:col + 256].reshape(KD, P, 256).transpose(1, 0, 2).reshape(P, KD * 256)

    blocks = []
    for j in range(AJ):
        blocks += [blk(w_in, at["x"] + 512 * j), blk(w_in, at["x"] + 512 * j + 256), blk(w_in, at["B"] + 256 * j),
                   blk(w_in, at["C"] + 256 * j), blk(w_in, at["z"] + 512 * j), blk(w_in, at["z"] + 512 * j + 256),
                   blk(w_in, at["pool"] + 256 * j), blk(w_in, at["gp"] + 256 * j)]
    so = a["ssm_out"][0]
    for q in range(4):
        blocks += [blk(w_in, at["gs"] + 256 * q), blk(so[0:D], 256 * q), blk(so[D:], 256 * q)]
    blocks += [blk(a["w_out"][0], 256 * n) for n in range(4)]
    blocks += [blk(a["w_q"][0], 256 * n) for n in range(PH)]

    def by_block(v):
        v = v.reshape(-1, 4096)
        cols = []
        for j in range(AJ):
            for c0 in (512 * j, 512 * j + 256, INNER + 256 * j, INNER + D + 256 * j):
                cols += [v[:, c0:c0 + P], v[:, c0 + P:c0 + 2 * P]]
        return np.stack(cols, 0).transpose(2, 0, 1)

    x = a["x"][0]
    arrays = {
        "x": x,
        "xt": x.T.reshape(KD, P, SEQ).transpose(1, 0, 2),
        "wblocks": np.stack(blocks),
        "wdt": w_in[:, at["dt"]:at["dt"] + HEADS].reshape(KD, P, HEADS).transpose(1, 0, 2),
        "poolw": a["pool_w"][0].reshape(4, 2, P, 256).transpose(0, 2, 1, 3),
        "pscale": a["pool_scale"][0].reshape(KD, P).T,
        "convw": by_block(a["conv_w"][0]),
        "convb": by_block(a["conv_b"][0])[:, :, 0],
        "dtb": a["dt_bias"], "alog": a["a_log"], "dskip": a["d_skip"],
        "normw": a["ssm_norm_w"][0].reshape(INNER // P, P).T,
        "ln1g": a["ln1_g"], "ln1b": a["ln1_b"], "ln2g": a["ln2_g"], "ln2b": a["ln2_b"],
        "subkt": a["sub_keys"][0].transpose(2, 0, 1),
        "eu": a["expert_u"][0], "ev": a["expert_v"][0],
    }
    arrays = {k: np.ascontiguousarray(v) for k, v in arrays.items()}
    nc = bacc.Bacc("TRN2", target_bir_lowering=False, num_devices=1)
    args = [nc.dram_tensor(k, v.shape, mybir.dt.from_np(v.dtype), kind="ExternalInput").ap() for k, v in arrays.items()]
    args.append(nc.dram_tensor("h_out", (SEQ, D), F32, kind="ExternalOutput").ap())
    build(nc, *args)
    r = run_bass_kernel_spmd(nc, [arrays], core_ids=[0])
    return np.asarray(r.results[0]["h_out"]).reshape(_OUT)
```

```python
from contextlib import ExitStack

import concourse.bass as bass
from concourse import mybir

ALU = mybir.AluOpType
ACT = mybir.ActivationFunctionType
AX = mybir.AxisListType
F32 = mybir.dt.float32
U32 = mybir.dt.uint32
ds = bass.ds

P = 128
SEQ = 1024
D = 1024
KD = D // P
T = 256
NT = T // P
NC = SEQ // T
WINDOWS = (2, 4, 8, 16)
HALO = 16
INNER = 2 * D
HEADS = 32
HD = 64
GROUPS = 8
HG = HEADS // GROUPS
GW = HG * HD
TAPS = 4
PH = 8
KEYS = 128
TOPK = 16
UNITS = NT * PH
NCAND = sum(TOPK // (i + 1) for i in range(TOPK))
ALPHA = 2.0 ** 0.25
EPS = 1e-5
NEG = -1e30
LOWEST = -3.4028234663852886e38

RING = 4
AJ = 4
BA, BC, BW, BD = 8 * AJ, 12, 4, 8
BLOCKS = BA + BC + BW + BD
MA, MC, MW, MD = 12, 8, 4, 8
MAINS = AJ * MA + MC + MW + MD
TA, TW, TD = 12, 4, 8
TURNS = AJ * TA + TW + TD
PE_ROWS = (2, 5, 8, 11)
VPE = len(PE_ROWS)
DVE_ROWS = tuple(k for k in range(TOPK) if k not in PE_ROWS)
UROWS = TOPK + len(DVE_ROWS)
ROWS = 7
TURNS_OF_ROWS = UROWS // ROWS


def build(nc, x, xt, wblocks, wdt, poolw, pscale, convw, convb, dtb, alog, dskip, normw,
          ln1g, ln1b, ln2g, ln2b, subkt, eu, ev, out):
    with ExitStack() as ctx:
        def sb(name, shape, dt=F32):
            return ctx.enter_context(nc.sbuf_tensor(name, shape, dt))

        def pb(name):
            return ctx.enter_context(nc.psum_tensor(name, [P, 512], F32))

        def sem(name):
            return ctx.enter_context(nc.semaphore(name))

        main = pb("main0"), pb("main1")
        turn = pb("turn0"), pb("turn1")
        ybank = pb("ybank")
        stbank = pb("stbank")
        vbank = pb("vbank0"), pb("vbank1")

        ring = [sb(f"ring{r}", [P, KD, 256]) for r in range(RING)]
        xT = sb("xT", [P, KD, T])
        pw = sb("pw", [P, 2, 256])
        wdt_s = sb("wdt_s", [P, KD, HEADS])
        subk = sb("subk", [P, 2, KEYS])
        lng2, lnb2 = sb("lng2", [P, D]), sb("lnb2", [P, D])
        cw = sb("cw", [P, AJ * 4 * 2, TAPS])
        cbias = sb("cbias", [P, AJ * 4 * 2])
        psc = sb("psc", [P, KD])
        nw = sb("nw", [P, INNER // P])
        dtb_s, a_s, dsk = sb("dtb_s", [P, HEADS]), sb("a_s", [P, HEADS]), sb("dsk", [P, HEADS])
        ident, upper, ones = sb("ident", [P, P]), sb("upper", [P, P]), sb("ones", [P, P])
        mask = sb("mask", [P, P])
        mask4 = mask[:, :].unsqueeze(1).to_broadcast([P, HG, P])
        zeros = sb("zeros", [P, P])
        iota = sb("iota", [P, NCAND])
        pcoef = sb("pcoef", [P, 4, 4])
        pfix = sb("pfix", [P, 4, 16])
        craw_ln1 = sb("craw_ln1", [P, 2 * 2 * (3 + T)])
        craw = craw_ln1[:, :].rearrange("p (b a t) -> p b a t", b=2, a=2)
        lng1 = craw_ln1[:, 0:D]
        cdiag = sb("cdiag", [P, 2, TAPS, P])
        cbs = cdiag[:, 0, :, :]
        lnb1 = cdiag[:, :, :, :].rearrange("p a k l -> p (a k l)")
        ctail = sb("ctail", [P, AJ * 4 * 2, 3])
        early = sb("early", [P, 2 * KD * P])
        xs = early[:, 0:4 * T].rearrange("p (c t) -> p c t", c=4)
        xtok = early[:, 4 * T:4 * T + NT * 512].rearrange("p (t c) -> p t c", t=NT)
        hT = early[:, :].rearrange("p (k t) -> p k t", k=KD)
        BT, CT = sb("BT", [P, 2, T]), sb("CT", [P, 2, T])
        btok = sb("btok", [P, NT, 256])
        zy = sb("zy", [P, 2 * NT * 512])
        zs = zy[:, 0:NT * 512].rearrange("p (t c) -> p t c", t=NT)
        yg = zy[:, NT * 512:].rearrange("p (t c) -> p t c", t=NT)
        xres = zy[:, :].rearrange("p (t c) -> p t c", t=NT)
        ptail = sb("ptail", [P, KD, HALO])
        merged = sb("merged", [P, KD, T])
        state = sb("state", [P, INNER])
        lexp = sb("lexp", [P, 2, HG, P])
        gps, asb = (lexp[:, b, :, :].rearrange("p h l -> p (h l)").rearrange("p (a t) -> p a t", a=2) for b in range(2))
        pooled = asb
        mm = sb("mm", [P, 2, HG, P])
        praw = mm[:, :, :, :].rearrange("p b h l -> p (b h l)")[:, 0:2 * (HALO + T)].rearrange("p (a t) -> p a t", a=2)
        scr = sb("scr", [P, 4 * (HALO + T)])
        psa, psb = (scr[:, a * 2 * (HALO + T):(a + 1) * 2 * (HALO + T)].rearrange("p (a t) -> p a t", a=2) for a in range(2))
        xd, xdd = (scr[:, a * 2 * GW:(a + 1) * 2 * GW].rearrange("p (b n) -> p b n", b=2) for a in range(2))
        yt1, yt2 = sb("yt1", [P, GW]), sb("yt2", [P, GW])
        NTH = NT * HEADS
        dtv, dte, dtu, dtl = (yt2[:, a * NTH:(a + 1) * NTH] for a in range(4))
        dt_ = sb("dt_", [P, NTH])
        adt = sb("adt", [P, NTH])
        adtc = sb("adtc", [P, NT, 2 * HG])
        nacum, eacum, dst, cdec = (sb(n, [P, NTH]) for n in ("nacum", "eacum", "dst", "cdec"))
        rms = sb("rms", [P, 4])
        rmsr = sb("rmsr", [P, 4])
        late = sb("late", [P, INNER // P * T])
        yT = late[:, :].rearrange("p (k t) -> p k t", k=INNER // P)
        qT = late[:, 0:1024].rearrange("p (b s t) -> p b s t", b=2, s=2)
        ssb = late[:, 1024:2048].rearrange("p (b r n) -> p b r n", b=2, r=4)
        sel1 = late[:, 2048:2048 + TOPK * NCAND].rearrange("p (k n) -> p k n", k=TOPK)
        snext = late[:, 2848:2848 + KEYS]
        bm = late[:, 2976:2976 + 128].rearrange("p (u k) -> p u k", u=8)
        posf = late[:, 3104:3104 + 128].rearrange("p (u k) -> p u k", u=8)
        self_ = late[:, 3232:3232 + 128].rearrange("p (u k) -> p u k", u=8)
        bex = late[:, 3360:3360 + 128].rearrange("p (u k) -> p u k", u=8)
        bsum = late[:, 3488:3488 + 8]
        cnext = late[:, 3496:3496 + NCAND]
        mflat = merged[:, :, :].rearrange("p k t -> p (k t)")
        tm = mflat[:, 0:256].rearrange("p (u s k) -> p u s k", u=8, s=2)
        tf = mflat[:, 256:512].rearrange("p (u s k) -> p u s k", u=8, s=2)
        cand = mflat[:, 512:512 + 8 * NCAND].rearrange("p (u n) -> p u n", u=8)
        candi = mflat[:, 912:912 + 8 * NCAND].rearrange("p (u n) -> p u n", u=8)
        tmi = sb("tmi", [P, 8, 2, TOPK], U32)
        pos = sb("pos", [P, 8, TOPK], U32)
        hf = sb("hf", [P, NT, D])
        stats, mv = sb("stats", [P, NT, 2, 6]), sb("mv", [P, NT, 2])
        lstd = sb("lstd", [P, NT])
        lrst = sb("lrst", [P, NT])
        idxf, gatef = sb("idxf", [P, UNITS, TOPK], U32), sb("gatef", [P, UNITS, TOPK])
        idxp, gatep = sb("idxp", [P, UNITS + 1, TOPK], U32), sb("gatep", [P, UNITS, TOPK])
        hp = sb("hp", [P, NT, D])
        icur = [sb(f"icur{b}", [P, TOPK], U32) for b in range(2)]
        hdot, hgel, hact = (sb(n, [P, 2, TOPK]) for n in ("hdot", "hgel", "hact"))
        rows = [sb(f"rows{r}", [P, D]) for r in range(ROWS)]
        rows_pe = [sb(f"rows_pe{i}", [P, D]) for i in range(VPE)]
        acc = sb("acc", [P, D])
        vdiag = sb("vdiag", [P, VPE, P])
        pstats, pmv = sb("pstats", [P, 2, 6]), sb("pmv", [P, 2])
        pstd, prst = sb("pstd", [P, 1]), sb("prst", [P, 1])

        const_dma = sem("const_dma")
        const_made = sem("const_made")
        dve_ready = sem("dve_ready")
        a_made = sem("a_made")
        w_ready = [sem(f"w_ready{r}") for r in range(RING)]
        block_done = sem("block_done")
        xt_ready = sem("xt_ready")
        pw_ready = sem("pw_ready")
        xres_ready = sem("xres_ready")
        main_free = sem("main_free")
        turn_ready = sem("turn_ready")
        turn_free = sem("turn_free")
        conv_raw = sem("conv_raw")
        pool_raw, pool_done = sem("pool_raw"), sem("pool_done")
        dt_proj, dt_abs, dt_exp, dt_u, dt_ln = (sem(n) for n in ("dt_proj", "dt_abs", "dt_exp", "dt_u", "dt_ln"))
        adt_ready, acum_ready, dec_in, dec_ready = (sem(n) for n in ("adt_ready", "acum_ready", "dec_in", "dec_ready"))
        adtc_ready = sem("adtc_ready")
        l_ready = sem("l_ready")
        m_done = sem("m_done")
        y_ready, y_free, st_ready, st_used = sem("y_ready"), sem("y_free"), sem("st_ready"), sem("st_used")
        rms_in, rms_sqrt, rms_rstd = sem("rms_in"), sem("rms_sqrt"), sem("rms_rstd")
        yn_ready = sem("yn_ready")
        pair_merged = sem("pair_merged")
        ln1_var, ln1_std, h_ready = sem("ln1_var"), sem("ln1_std"), sem("h_ready")
        topk_done = sem("topk_done")
        sm_in, sm_exp = sem("sm_in"), sem("sm_exp")
        idx_ready = sem("idx_ready")
        row_ready = [sem(f"row_ready{r}") for r in range(ROWS)]
        row_ready_pe = [sem(f"row_ready_pe{i}") for i in range(VPE)]
        row_free, row_free_pe = sem("row_free"), sem("row_free_pe")
        hact_ready, vdiag_ready, vsum_read = sem("hact_ready"), sem("vdiag_ready"), sem("vsum_read")
        gelu_ready = sem("gelu_ready")
        ln2_var, ln2_std, out_ready, out_done = (sem(n) for n in ("ln2_var", "ln2_std", "out_ready", "out_done"))

        BANKS = 2
        DECAYS = (7, 8, 10, 11)
        TURNED = 10
        CONV = (0, 1, 3, 4)
        STATE = 1
        NCONST = 10

        def spread(ap, n):
            s = list(ap.shape)
            return ap.unsqueeze(len(s)).to_broadcast(s + [n])

        def heads(table, t, j, gg):
            return table[:, ds(t * HEADS + j * 2 * HG + gg * HG, HG)]

        def weave(slots, front, per_slot=1, after=0, rest=True):
            for n, _ in enumerate(slots):
                if n >= after:
                    for _ in range(per_slot):
                        next(front, None)
            if rest:
                for _ in front:
                    pass

        def emptied(eng, c, m):
            eng.wait_ge(main_free, c * MAINS + m + BANKS)

        def unturned(eng, c, m):
            eng.wait_ge(turn_free, c * TURNS + m + BANKS)

        block = ctx.enter_context(nc.Block())

        @block.sync
        def _(sp):
            for dst_, src in ((wdt_s[:, :, :], wdt), (subk[:, :, :], subkt), (cw[:, :, :], convw),
                              (cbias[:, :], convb), (psc[:, :], pscale), (nw[:, :], normw),
                              (dtb_s[:, :], dtb.to_broadcast([P, HEADS])),
                              (a_s[:, :], alog.to_broadcast([P, HEADS])),
                              (dsk[:, :], dskip.to_broadcast([P, HEADS])),
                              (lng2[:, :], ln2g.to_broadcast([P, D]))):
                sp.dma_start(dst_, src).then_inc(const_dma, 16)

            def load_blocks(c, b):
                for r in range(RING):
                    sp.wait_ge(block_done, c * BLOCKS + b + r + 1)
                    sp.dma_start(ring[r][:, :, :], wblocks[ds(b + r, 1), :, :].rearrange("o p (k n) -> (o p) k n", k=KD)
                                 ).then_inc(w_ready[r], 16)

            def load_xt(c):
                sp.dma_start(xT[:, :, :], xt[:, :, ds(c * T, T)]).then_inc(xt_ready, 16)

            def superchunk(c):
                with sp.Fori(0, AJ) as j:
                    load_blocks(c, j * 8)
                    sp.wait_ge(turn_ready, c * TURNS + (j - 1) * TA + 3 + TURNED)
                    sp.dma_start(pw[:, :, :], poolw[ds(j, 1), :, :, :].rearrange("o p k n -> (o p) k n")
                                 ).then_inc(pw_ready, 16)
                    load_blocks(c, j * 8 + 4)
                with sp.Fori(0, 2) as m:
                    load_blocks(c, BA + m * 4)
                sp.wait_ge(turn_ready, c * TURNS + AJ * TA + TURNED)
                sp.dma_start(xres, x[ds(c * T, T), :].rearrange("(t p) d -> p t d", p=P)).then_inc(xres_ready, 16)
                sp.dma_start(lng1, ln1g.to_broadcast([P, D])).then_inc(xres_ready, 16)
                sp.dma_start(lnb1, ln1b.to_broadcast([P, D])).then_inc(xres_ready, 16)
                with sp.Fori(0, 2) as m:
                    load_blocks(c, BA + 8 + m * 4)
                sp.wait_ge(block_done, c * BLOCKS + BA + BC + RING)

            def rest(c):
                with sp.Fori(0, 2) as m:
                    load_blocks(c, BA + 16 + m * 4)

            load_xt(0)
            with sp.Fori(0, NC - 1) as c:
                superchunk(c)
                load_xt(c + 1)
                rest(c)
            superchunk(NC - 1)
            load_xt(NC - 1)
            rest(NC - 1)

        @block.gpsimd
        def _(pool):
            pool.memset(ones[:, :], 1.0).then_inc(const_made, 1)
            pool.memset(mask[:, :], 0.0).then_inc(const_made, 1)
            pool.wait_ge(const_dma, 16 * NCONST)
            pool.memset(ident[:, :], 0.0).then_inc(const_made, 1)
            pool.wait_ge(const_made, 3)
            pool.affine_select(out=ident[:, :], in_=ident[:, :], compare_op=ALU.not_equal, fill=1.0, base=0,
                               pattern=[[1, P]], channel_multiplier=-1).then_inc(const_made, 1)
            pool.affine_select(out=upper[:, :], in_=ones[:, :], compare_op=ALU.is_ge, fill=0.0, base=0,
                               pattern=[[1, P]], channel_multiplier=-1).then_inc(const_made, 1)
            pool.affine_select(out=mask[:, :], in_=mask[:, :], compare_op=ALU.is_ge, fill=NEG, base=0,
                               pattern=[[1, P]], channel_multiplier=-1).then_inc(const_made, 1)
            pool.iota(iota[:, :], pattern=[[1, NCAND]], base=0, channel_multiplier=0,
                      allow_small_or_imprecise_dtypes=True).then_inc(const_made, 1)
            for w in range(4):
                pool.iota(pfix[:, w, :], pattern=[[1, 16]], base=1, channel_multiplier=0,
                          allow_small_or_imprecise_dtypes=True).then_inc(const_made, 1)

            by_dve, by_pe = pool.alloc_register("rows_by_dve"), pool.alloc_register("rows_by_pe")
            pool.reg_mov(by_dve, 1)
            pool.reg_mov(by_pe, 1)
            with pool.Fori(0, NC * UNITS // 2) as pair:
                for b in range(2):
                    n_dve = 0
                    for table in (eu, ev):
                        for k in range(TOPK):
                            if table is ev and k in PE_ROWS:
                                i = PE_ROWS.index(k)
                                count, used, dst_, landed = by_pe, row_free_pe, rows_pe[i], row_ready_pe[i]
                            else:
                                r = n_dve % ROWS
                                n_dve += 1
                                count, used, dst_, landed = by_dve, row_free, rows[r], row_ready[r]
                            n = pool.snap(count)
                            if table is eu and k == 0:
                                pool.wait_ge(idx_ready, pair * 2 + b + 1)
                            pool.wait_ge(used, n)
                            pool.reg_add(count, count, 1)
                            pool.indirect_dma_start(dst_[:, :], None, table,
                                                    bass.IndirectOffsetOnAxis(ap=icur[b][:, k:k + 1], axis=0)
                                                    ).then_inc(landed, 16)

        @block.tensor
        def _(pe):
            def block_in(c, turns, n):
                pe.wait_ge(w_ready[n % RING], (c * (BLOCKS // RING) + turns + n // RING + 1) * 16)
                return ring[n % RING]

            def bank(c, m, n):
                pe.wait_ge(main_free, c * MAINS + m + n + 1)
                return main[n % 2]

            def turn_bank(c, m, n):
                pe.wait_ge(turn_free, c * TURNS + m + n + 1)
                return turn[n % 2]

            def channels(dst_, w, src):
                for ct in range(2):
                    for k in range(KD):
                        last = pe.matmul(dst_[:, ct * T:(ct + 1) * T], w[:, k, ct * P:(ct + 1) * P], src[:, k, :],
                                         start=(k == 0), stop=(k == KD - 1))
                return last

            def tokens(dst_, w, src):
                for t in range(NT):
                    for k in range(KD):
                        last = pe.matmul(dst_[:, t * 256:(t + 1) * 256], src[:, k, t * P:(t + 1) * P], w[:, k, :],
                                         start=(k == 0), stop=(k == KD - 1))
                return last

            def dt_product(c):
                pe.wait_ge(xt_ready, (c + 1) * 16)
                pe.wait_ge(st_used, c * 4 * AJ + STATE)
                for t in range(NT):
                    for k in range(KD):
                        last = pe.matmul(stbank[:, 256 + t * HEADS:256 + (t + 1) * HEADS], xT[:, k, t * P:(t + 1) * P],
                                         wdt_s[:, k, :], start=(k == 0), stop=(k == KD - 1))
                last.then_inc(dt_proj, 1)

            def dt_sums(c):
                pe.wait_ge(adt_ready, c + 1)
                pe.matmul(stbank[:, 320:320 + NTH], upper[:, :], adt[:, :], start=True, stop=True)
                pe.matmul(stbank[:, 384:384 + NTH], ones[:, :], adt[:, :], start=True, stop=True).then_inc(acum_ready, 1)

            def scan_scores(c, j, s):
                t, gg = s // 2, s % 2
                lbank = bank(c, j * MA, DECAYS[s])
                pe.matmul(lbank[:, :], ident[:, :], mask4, start=True, stop=False,
                          skip_group_check=True)
                for h in range(HG):
                    last = pe.matmul(lbank[:, h * P:(h + 1) * P],
                                     adtc[:, t, gg * HG + h:gg * HG + h + 1].to_broadcast([P, P]), upper[:, :],
                                     start=False, stop=(h == HG - 1), skip_group_check=True)
                last.then_inc(l_ready, 1)

            def scan_outputs(c, j, s):
                t, gg = s // 2, s % 2
                n = c * 4 * AJ + j * 4 + s
                pe.wait_ge(m_done, n + 3)
                pe.wait_ge(y_free, n + 1)
                if s >= 2:
                    pe.wait_ge(st_used, n - 1 + STATE)
                pe.matmul(ybank[:, GW:2 * GW], CT[:, gg, t * P:(t + 1) * P],
                          state[:, ds(j * 2 * GW + gg * GW, GW)], start=True, stop=True)
                for h in range(HG):
                    last = pe.matmul(ybank[:, h * HD:(h + 1) * HD], mm[:, s % 2, h, :],
                                     xd[:, s % 2, h * HD:(h + 1) * HD], start=True, stop=True)
                last.then_inc(y_ready, 1)
                pe.wait_ge(st_used, n + STATE)
                pe.matmul(stbank[:, 0:GW], btok[:, t, gg * P:(gg + 1) * P], xdd[:, s % 2, :],
                          start=True, stop=True).then_inc(st_ready, 1)

            def convolve(c, j, n):
                pe.wait_ge(conv_raw, c * 4 * AJ + j * 4 + n + 1)
                dst_ = turn_bank(c, j * TA, CONV[n])
                for ct in range(2):
                    for k in range(TAPS):
                        last = pe.matmul(dst_[:, ct * T:(ct + 1) * T], cdiag[:, ct, k, :], craw[:, n % 2, ct, k:k + T],
                                         start=(k == 0), stop=(k == TAPS - 1))
                last.then_inc(turn_ready, 1)

            def open_sums(c, t):
                pe.wait_ge(vsum_read, c * NT + t + 1)
                for half in range(2):
                    pe.matmul(vbank[half][:, :], zeros[:, :], mask4,
                              start=True, stop=False, skip_group_check=True)

            def sums(c, u, b):
                for i in range(VPE):
                    pe.wait_ge(vdiag_ready, (c * UNITS + u) * VPE + i + 1)
                    pe.wait_ge(row_ready_pe[i], (c * UNITS + u + 1) * 16)
                    for half in range(2):
                        last = pe.matmul(vbank[half][:, :], vdiag[:, i, :], rows_pe[i][:, half * 512:(half + 1) * 512],
                                         start=False, stop=False, skip_group_check=True)
                    last.then_inc(row_free_pe, 1)

            def front_a1(c, j):
                for n in range(7):
                    w = block_in(c, j * (8 // RING), n)
                    dst_ = bank(c, j * MA, n)
                    (tokens if n == 6 else channels)(dst_, w, xT).then_inc(block_done, 1)
                    if n >= 3:
                        convolve(c, j, n - 3)
                    if n == 4:
                        pe.wait_ge(pw_ready, (c * AJ + j + 1) * 16)
                        pe.wait_ge(pool_done, c * AJ + j + 1)
                        dst_ = turn_bank(c, j * TA, 2)
                        for ct in range(2):
                            for k in range(2):
                                last = pe.matmul(dst_[:, ct * T:(ct + 1) * T], pw[:, k, ct * P:(ct + 1) * P],
                                                 pooled[:, k, :], start=(k == 0), stop=(k == 1))
                        last.then_inc(turn_ready, 1)

            def front_a2(c, j):
                unturned(pe, c, j * TA + 2)
                for t in range(NT):
                    dst_ = turn_bank(c, j * TA, 5 + t)
                    for ct in range(4):
                        last = pe.transpose(dst_[:, ct * P:(ct + 1) * P], xs[:, ct, t * P:(t + 1) * P], ident[:, :])
                    last.then_inc(turn_ready, 1)
                unturned(pe, c, j * TA + 5)
                dst_ = turn_bank(c, j * TA, 7)
                for t in range(NT):
                    for ct in range(2):
                        last = pe.transpose(dst_[:, t * 256 + ct * P:t * 256 + (ct + 1) * P],
                                            BT[:, ct, t * P:(t + 1) * P], ident[:, :])
                last.then_inc(turn_ready, 1)
                for t in range(NT):
                    dst_ = turn_bank(c, j * TA, 8 + t)
                    for gg in range(2):
                        last = pe.matmul(dst_[:, gg * P:(gg + 1) * P], BT[:, gg, t * P:(t + 1) * P],
                                         CT[:, gg, t * P:(t + 1) * P], start=True, stop=True)
                    last.then_inc(turn_ready, 1)
                pe.wait_ge(adtc_ready, c * AJ + j + 1)
                unturned(pe, c, j * TA + 8)
                scan_scores(c, j, 0)
                for s in range(4):
                    if s < 3:
                        scan_scores(c, j, s + 1)
                    scan_outputs(c, j, s)
                    if s == 0:
                        w = block_in(c, j * (8 // RING), 7)
                        tokens(bank(c, j * MA, 9), w, xT).then_inc(block_done, 1)

            def front_a3(c, j):
                pe.wait_ge(yn_ready, c * AJ + j + 1)
                for gg in range(2):
                    dst_ = turn_bank(c, j * TA, 10 + gg)
                    for ct in range(2):
                        for t in range(NT):
                            last = pe.transpose(dst_[:, ct * T + t * P:ct * T + (t + 1) * P],
                                                yg[:, t, gg * GW + ct * P:gg * GW + (ct + 1) * P], ident[:, :])
                    last.then_inc(turn_ready, 1)

            def front_pair(c, q):
                if q == 0:
                    unturned(pe, c, AJ * TA)
                w = block_in(c, BA // RING, 3 * q)
                dst_ = bank(c, AJ * MA, 2 * q)
                channels(dst_, w, xT).then_inc(block_done, 1)
                lo, hi = block_in(c, BA // RING, 3 * q + 1), block_in(c, BA // RING, 3 * q + 2)
                dst_ = bank(c, AJ * MA, 2 * q + 1)
                for ct in range(2):
                    for k in range(2 * KD):
                        last = pe.matmul(dst_[:, ct * T:(ct + 1) * T], (lo, hi)[k // KD][:, k % KD, ct * P:(ct + 1) * P],
                                         yT[:, k, :], start=(k == 0), stop=(k == 2 * KD - 1))
                last.then_inc(block_done, 2)

            def front_w(c):
                pe.wait_ge(pair_merged, (c + 1) * 4)
                for n in range(4):
                    w = block_in(c, (BA + BC) // RING, n)
                    dst_ = bank(c, AJ * MA + MC, n)
                    tokens(dst_, w, merged).then_inc(block_done, 1)
                pe.wait_ge(h_ready, c + 1)
                for n in range(4):
                    dst_ = turn_bank(c, AJ * TA, n)
                    for ct in range(2):
                        for t in range(NT):
                            last = pe.transpose(dst_[:, ct * T + t * P:ct * T + (t + 1) * P],
                                                hf[:, t, (2 * n + ct) * P:(2 * n + ct + 1) * P], ident[:, :])
                    last.then_inc(turn_ready, 1)

            def front_d(c, i):
                def query(hh):
                    w = block_in(c, (BA + BC + BW) // RING + i, hh)
                    dst_ = bank(c, AJ * MA + MC + MW + i * 4, hh)
                    channels(dst_, w, hT).then_inc(block_done, 1)

                def score(hh):
                    emptied(pe, c, AJ * MA + MC + MW + i * 4 + hh + 1)
                    dst_ = turn_bank(c, AJ * TA + TW + i * 4, hh)
                    for t in range(NT):
                        for side in range(2):
                            n = t * 2 + side
                            last = pe.matmul(dst_[:, n * KEYS:(n + 1) * KEYS], qT[:, hh % 2, side, t * P:(t + 1) * P],
                                             subk[:, side, :], start=True, stop=True)
                    last.then_inc(turn_ready, 1)

                unturned(pe, c, AJ * TA + TW)
                query(0)
                for hh in range(4):
                    if hh < 3:
                        query(hh + 1)
                    score(hh)

            pe.sem_inc(block_done, RING)
            pe.sem_inc(turn_ready, TURNED)
            pe.sem_inc(row_free_pe, VPE)
            pe.wait_ge(const_dma, 16 * NCONST)
            pe.wait_ge(const_made, 11)
            pe.wait_ge(dve_ready, 1)

            def superchunk(cf, cp):
                f, e = cf is not None, cp is not None
                if e:
                    open_sums(cp, 0)
                with pe.Fori(0, AJ) as j:
                    if f:
                        front_a1(cf, j)
                    if e:
                        sums(cp, j * 2, 0)
                    if f:
                        front_a2(cf, j)
                    if e:
                        sums(cp, j * 2 + 1, 1)
                    if f:
                        front_a3(cf, j)
                if e:
                    open_sums(cp, 1)
                for i in range(2):
                    if f:
                        front_pair(cf, 2 * i)
                        front_pair(cf, 2 * i + 1)
                    if e:
                        sums(cp, 8 + i, i)
                if f:
                    front_w(cf)
                    dt_product(cf + 1)
                if e:
                    sums(cp, 10, 0)
                if f:
                    dt_sums(cf + 1)
                if e:
                    sums(cp, 11, 1)
                with pe.Fori(0, 2) as i:
                    if f:
                        front_d(cf, i)
                    if e:
                        for b in range(2):
                            sums(cp, 12 + i * 2 + b, b)

            dt_product(0)
            dt_sums(0)
            superchunk(0, None)
            with pe.Fori(0, NC - 1) as c:
                superchunk(c + 1, c)
            superchunk(None, NC - 1)

        @block.scalar
        def _(act):
            def filled(c, blocks, m):
                act.wait_ge(block_done, c * BLOCKS + blocks + RING)
                return main[m % 2]

            def turned(c, m, n):
                act.wait_ge(turn_ready, c * TURNS + m + n + 1 + TURNED)
                return turn[n % 2]

            def silu_conv(c, j, n):
                src = turned(c, j * TA, CONV[n])
                dst_ = (xs[:, 0:2, :], xs[:, 2:4, :], BT[:, :, :], CT[:, :, :])[n]
                for ct in range(2):
                    last = act.activation(dst_[:, ct, :], src[:, ct * T:(ct + 1) * T], ACT.Silu,
                                          bias=cbias[:, ds(j * 8 + n * 2 + ct, 1)])
                last.then_inc(turn_free, 1)

            def conv_weights(c, j, n):
                for ct in range(2):
                    for k in range(TAPS):
                        last = act.activation(cdiag[:, ct, k, :], ident[:, :], ACT.Copy,
                                              scale=cw[:, ds(j * 8 + n * 2 + ct, 1), k:k + 1].rearrange("p a b -> p (a b)"))
                last.then_inc(conv_raw, 1)

            def raw_conv(c, j, n):
                src = filled(c, j * 8 + n + 3, n)[:, :].rearrange("p (a t) -> p a t", a=2)
                tail = ctail[:, ds(j * 8 + n * 2, 2), :]
                act.copy(craw[:, n % 2, :, 3:3 + T], src).then_inc(main_free, 1)
                act.copy(craw[:, n % 2, :, 0:3], tail)
                act.drain()
                act.copy(tail, craw[:, n % 2, :, T:T + 3])

            def front_dt(c):
                act.wait_ge(dt_abs, c + 1)
                act.activation(dte[:, :], dte[:, :], ACT.Exp).then_inc(dt_exp, 1)
                act.wait_ge(dt_u, c + 1)
                act.activation(dtl[:, :], dtu[:, :], ACT.Ln).then_inc(dt_ln, 1)
                act.wait_ge(dec_in, c + 1)
                act.activation(dst[:, :], dst[:, :], ACT.Exp)
                act.activation(eacum[:, :], stbank[:, 320:320 + NTH], ACT.Exp)
                act.activation(cdec[:, :], stbank[:, 384:384 + NTH], ACT.Exp).then_inc(dec_ready, 1)

            def front_a1(c, j):
                src = filled(c, j * 8 + 1, 0)[:, :].rearrange("p (a t) -> p a t", a=2)
                tail = ptail[:, ds(j * 2, 2), :]
                act.copy(praw[:, :, HALO:], src).then_inc(main_free, 1)
                act.copy(praw[:, :, 0:HALO], tail)
                act.drain()
                act.copy(tail, praw[:, :, T:T + HALO]).then_inc(pool_raw, 1)
                src = filled(c, j * 8 + 2, 1)[:, :].rearrange("p (a t) -> p a t", a=2)
                act.activation(gps, src, ACT.Sigmoid).then_inc(main_free, 1)
                raw_conv(c, j, 0)
                conv_weights(c, j, 0)
                raw_conv(c, j, 1)
                silu_conv(c, j, 0)
                conv_weights(c, j, 1)

            def silu_z(c, j, g):
                src = filled(c, j * 8 + 7 + g, 6 + 3 * g)[:, :].rearrange("p (t n) -> p t n", t=NT)
                act.activation(zs[:, :, g * GW:(g + 1) * GW], src, ACT.Silu).then_inc(main_free, 1)

            def front_a2(c, j):
                raw_conv(c, j, 2)
                silu_conv(c, j, 1)
                conv_weights(c, j, 2)
                src = turned(c, j * TA, 2)
                for ct in range(2):
                    last = act.activation(asb[:, ct, :], src[:, ct * T:(ct + 1) * T], ACT.Copy,
                                          scale=psc[:, ds(j * 2 + ct, 1)])
                last.then_inc(turn_free, 1)
                raw_conv(c, j, 3)
                silu_conv(c, j, 2)
                conv_weights(c, j, 3)
                silu_z(c, j, 0)
                silu_conv(c, j, 3)
                for t in range(NT):
                    act.copy(xtok[:, t, :], turned(c, j * TA, 5 + t)[:, :]).then_inc(turn_free, 1)
                act.copy(btok[:, :, :], turned(c, j * TA, 7)[:, :].rearrange("p (t n) -> p t n", t=NT)
                         ).then_inc(turn_free, 1)
                for t in range(NT):
                    act.copy(cbs[:, 2 * t:2 * t + 2, :],
                             turned(c, j * TA, 8 + t)[:, 0:2 * P].rearrange("p (g l) -> p g l", g=2)).then_inc(turn_free, 1)

            def decays(c, j, s):
                n = c * 4 * AJ + j * 4 + s
                act.wait_ge(l_ready, n + 1)
                act.wait_ge(m_done, n + 1)
                t, gg = s // 2, s % 2
                lbank = main[DECAYS[s] % 2]
                for h in range(HG):
                    last = act.activation(lexp[:, s % 2, h, :], lbank[:, h * P:(h + 1) * P], ACT.Exp,
                                          bias=nacum[:, ds(t * HEADS + j * 2 * HG + gg * HG + h, 1)])
                last.then_inc(main_free, 1)

            def front_a3(c, j):
                for s in range(4):
                    decays(c, j, s)
                    if s == 1:
                        silu_z(c, j, 1)
                act.wait_ge(rms_in, c * AJ + j + 1)
                act.activation(rms[:, :], rms[:, :], ACT.Sqrt).then_inc(rms_sqrt, 1)
                act.wait_ge(rms_rstd, c * AJ + j + 1)
                for s in range(4):
                    y = yg[:, s // 2, (s % 2) * GW:(s % 2 + 1) * GW]
                    last = act.activation(y, y, ACT.Copy, scale=rmsr[:, s:s + 1])
                last.then_inc(yn_ready, 1)
                for gg in range(2):
                    src = turned(c, j * TA, 10 + gg)
                    for ct in range(2):
                        k = j * 4 + gg * 2 + ct
                        last = act.activation(yT[:, ds(k, 1), :], src[:, ct * T:(ct + 1) * T].unsqueeze(1), ACT.Copy,
                                              scale=nw[:, ds(k, 1)])
                    last.then_inc(turn_free, 1)

            def front_pair(c, q):
                if q >= 2:
                    act.wait_ge(pair_merged, c * 4 + q - 1)
                flat = lexp[:, q % 2, :, :].rearrange("p a b -> p (a b)")
                act.activation(flat, filled(c, BA + 3 * q + 1, 0)[:, :], ACT.Sigmoid).then_inc(main_free, 1)
                flat = mm[:, q % 2, :, :].rearrange("p a b -> p (a b)")
                act.copy(flat, filled(c, BA + 3 * q + 3, 1)[:, :]).then_inc(main_free, 1)

            def front_w(c):
                for n in range(4):
                    src = filled(c, BA + BC + n + 1, n)[:, :].rearrange("p (t n) -> p t n", t=NT)
                    act.copy(hf[:, :, n * 256:(n + 1) * 256], src).then_inc(main_free, 1)

            def front_ln1(c):
                act.wait_ge(ln1_var, c + 1)
                act.activation(lstd[:, :], lstd[:, :], ACT.Sqrt).then_inc(ln1_std, 1)
                for n in range(4):
                    src = turned(c, AJ * TA, n)[:, :].rearrange("p (a t) -> p a t", a=2)
                    act.copy(hT[:, 2 * n:2 * n + 2, :], src).then_inc(turn_free, 1)

            def front_d(c, i, half):
                def query(hh):
                    src = filled(c, BA + BC + BW + i * 4 + hh + 1, hh)[:, :].rearrange("p (a t) -> p a t", a=2)
                    act.copy(qT[:, hh % 2, :, :], src).then_inc(main_free, 1)

                def score(hh):
                    src = turned(c, AJ * TA + TW + i * 4, hh)[:, :].rearrange("p (a n) -> p a n", a=4)
                    act.wait_ge(topk_done, c * PH + i * 4 + hh + 1)
                    act.copy(ssb[:, hh % 2, :, :], src).then_inc(turn_free, 1)

                if half == 0:
                    query(0)
                    query(1)
                    score(0)
                    query(2)
                    score(1)
                elif half == 1:
                    query(3)
                    score(2)
                    score(3)
                elif half == 3:
                    act.wait_ge(sm_in, c * 2 + i + 1)
                    act.activation(bex, bex, ACT.Exp).then_inc(sm_exp, 1)

            def gates(c, u, b):
                act.wait_ge(row_free, (c * UNITS + u) * UROWS + TOPK + ROWS)
                act.activation(hgel[:, b, :], hdot[:, b, :], ACT.Gelu).then_inc(gelu_ready, 1)
                act.wait_ge(hact_ready, c * UNITS + u + 1)
                act.wait_ge(row_free_pe, (c * UNITS + u) * VPE + VPE)
                for i, k in enumerate(PE_ROWS):
                    act.activation(vdiag[:, i, :], ident[:, :], ACT.Copy, scale=hact[:, b, k:k + 1]).then_inc(vdiag_ready, 1)

            def finish_tile(c, t):
                act.wait_ge(ln2_var, c * NT + t + 1)
                act.activation(pstd[:, :], pstd[:, :], ACT.Sqrt).then_inc(ln2_std, 1)
                act.wait_ge(out_ready, c * NT + t + 1)
                act.dma_start(out[ds(c * T + t * P, P), :], acc[:, :]).then_inc(out_done, 16)

            def superchunk(cf, cp):
                with act.Fori(0, AJ) as j:
                    if cf is not None:
                        front_a1(cf, j)
                    if cp is not None:
                        gates(cp, j * 2, 0)
                    if cf is not None:
                        front_a2(cf, j)
                    if cp is not None:
                        gates(cp, j * 2 + 1, 1)
                    if cf is not None:
                        front_a3(cf, j)
                if cp is not None:
                    finish_tile(cp, 0)
                for i in range(2):
                    if cf is not None:
                        front_pair(cf, 2 * i)
                    if cp is not None:
                        gates(cp, 8 + i, i)
                    if cf is not None:
                        front_pair(cf, 2 * i + 1)
                if cf is not None:
                    front_w(cf)
                if cp is not None:
                    gates(cp, 10, 0)
                if cf is not None:
                    front_ln1(cf)
                    front_dt(cf + 1)
                if cp is not None:
                    gates(cp, 11, 1)
                with act.Fori(0, 2) as i:
                    for b in range(2):
                        if cf is not None:
                            front_d(cf, i, 2 * b)
                        if cp is not None:
                            gates(cp, 12 + i * 2 + b, b)
                        if cf is not None:
                            front_d(cf, i, 2 * b + 1)
                if cp is not None:
                    finish_tile(cp, 1)

            act.dma_start(lnb2[:, :], ln2b.to_broadcast([P, D])).then_inc(out_done, 16)
            act.sem_inc(main_free, BANKS)
            act.sem_inc(turn_free, BANKS)
            act.wait_ge(const_dma, 16 * NCONST)
            act.activation(a_s[:, :], a_s[:, :], ACT.Exp).then_inc(a_made, 1)
            act.wait_ge(dve_ready, 1)
            front_dt(0)
            superchunk(0, None)
            with act.Fori(0, NC - 1) as c:
                superchunk(c + 1, c)
            superchunk(None, NC - 1)
            act.wait_ge(out_done, 16 * (NC * NT + 1))

        @block.vector
        def _(dve):
            def front_dt(c):
                dve.wait_ge(dt_proj, c + 1)
                dve.tensor_tensor(dtv[:, :].rearrange("p (t h) -> p t h", t=NT),
                                  stbank[:, 256:256 + NTH].rearrange("p (t h) -> p t h", t=NT),
                                  dtb_s[:, :].unsqueeze(1).to_broadcast([P, NT, HEADS]), ALU.add)
                dve.drain()
                dve.tensor_scalar(dtu[:, :], dtv[:, :], -1.0, None, ALU.mult)
                dve.drain()
                dve.tensor_tensor(dte[:, :], dtv[:, :], dtu[:, :], ALU.min).then_inc(dt_abs, 1)
                yield
                dve.wait_ge(dt_exp, c + 1)
                dve.tensor_scalar(dtu[:, :], dte[:, :], 1.0, None, ALU.add).then_inc(dt_u, 1)
                dve.drain()
                dve.tensor_scalar(dt_[:, :], dtu[:, :], -1.0, None, ALU.add)
                dve.reciprocal(adt[:, :], dtu[:, :])
                dve.drain()
                dve.tensor_tensor(dte[:, :], dte[:, :], dt_[:, :], ALU.subtract)
                dve.drain()
                dve.tensor_tensor(dte[:, :], dte[:, :], adt[:, :], ALU.mult)
                dve.drain()
                yield
                dve.wait_ge(dt_ln, c + 1)
                dve.tensor_tensor(dtl[:, :], dtl[:, :], dte[:, :], ALU.add)
                dve.drain()
                dve.scalar_tensor_tensor(out=dt_[:, :], in0=dtv[:, :], scalar=0.0, in1=dtl[:, :],
                                         op0=ALU.max, op1=ALU.add)
                dve.drain()
                dve.tensor_tensor(adt[:, :].rearrange("p (t h) -> p t h", t=NT),
                                  dt_[:, :].rearrange("p (t h) -> p t h", t=NT),
                                  a_s[:, :].unsqueeze(1).to_broadcast([P, NT, HEADS]), ALU.mult).then_inc(adt_ready, 1)
                yield
                dve.wait_ge(acum_ready, c + 1)
                dve.tensor_scalar(nacum[:, :], stbank[:, 320:320 + NTH], -1.0, None, ALU.mult)
                dve.drain()
                dve.tensor_tensor(dst[:, :], stbank[:, 384:384 + NTH], nacum[:, :], ALU.add).then_inc(dec_in, 1)
                yield
                dve.wait_ge(dec_ready, c + 1)
                dve.tensor_tensor(dst[:, :], dst[:, :], dt_[:, :], ALU.mult)
                dve.drain()

            def pooling(c, j, first):
                dve.wait_ge(pool_raw, c * AJ + j + 1)
                E = HALO + T
                src, dst_, reach = praw, psa, 1
                for w in range(4):
                    lo = 2 * reach - 1
                    dve.tensor_tensor(dst_[:, :, lo:E], src[:, :, lo:E], src[:, :, lo - reach:E - reach], ALU.add)
                    dve.drain()
                    fixed = dst_[:, :, HALO:E]
                    if first:
                        fixed = yt1[:, 0:32].rearrange("p (a t) -> p a t", a=2)
                        dve.tensor_tensor(fixed, dst_[:, :, HALO:HALO + 16],
                                          pfix[:, w, :].unsqueeze(1).to_broadcast([P, 2, 16]), ALU.mult)
                        dve.drain()
                        spans = ((fixed, slice(0, 16)), (dst_[:, :, HALO + 16:E], slice(16, T)))
                    else:
                        spans = ((fixed, slice(0, T)),)
                    coef = pcoef[:, ds(j, 1), w:w + 1].rearrange("p a b -> p (a b)")
                    for s, to in spans:
                        o = pooled[:, :, to]
                        if w == 0:
                            raw = praw[:, :, HALO + to.start:HALO + to.stop]
                            last = dve.scalar_tensor_tensor(out=o, in0=s, scalar=coef, in1=raw,
                                                            op0=ALU.mult, op1=ALU.subtract)
                        else:
                            last = dve.scalar_tensor_tensor(out=o, in0=s, scalar=coef, in1=o,
                                                            op0=ALU.mult, op1=ALU.add)
                    if w == 3:
                        last.then_inc(pool_done, 1)
                    dve.drain()
                    src, dst_, reach = dst_, (psb if dst_ is psa else psa), 2 * reach
                    yield

            def merge_pool(c, j):
                unturned(dve, c, j * TA + 3)
                dve.tensor_tensor(merged[:, ds(j * 2, 2), :], asb, gps, ALU.mult)
                for t in range(NT):
                    last = dve.tensor_copy(adtc[:, t, :], adt[:, ds(t * HEADS + j * 2 * HG, 2 * HG)])
                last.then_inc(adtc_ready, 1)
                yield

            def scan_pre(c, j, s):
                t, gg = s // 2, s % 2
                n = c * 4 * AJ + j * 4 + s
                xv = xtok[:, t, gg * GW:(gg + 1) * GW].rearrange("p (h d) -> p h d", h=HG)
                dve.tensor_tensor(xd[:, s % 2, :].rearrange("p (h d) -> p h d", h=HG), xv,
                                  spread(heads(dt_, t, j, gg), HD), ALU.mult)
                dve.tensor_tensor(xdd[:, s % 2, :].rearrange("p (h d) -> p h d", h=HG), xv,
                                  spread(heads(dst, t, j, gg), HD), ALU.mult)
                yield
                emptied(dve, c, j * MA + DECAYS[s] + 1)
                dve.tensor_tensor(mm[:, s % 2, :, :], lexp[:, s % 2, :, :],
                                  cbs[:, s, :].unsqueeze(1).to_broadcast([P, HG, P]), ALU.mult).then_inc(m_done, 1)
                yield

            def scan_post(c, j, s):
                t, gg = s // 2, s % 2
                n = c * 4 * AJ + j * 4 + s
                xv = xtok[:, t, gg * GW:(gg + 1) * GW].rearrange("p (h d) -> p h d", h=HG)
                y3 = yt1[:, :].rearrange("p (h d) -> p h d", h=HG)
                dve.drain()
                dve.tensor_tensor(yt2[:, :].rearrange("p (h d) -> p h d", h=HG), xv,
                                  spread(dsk[:, ds(j * 2 * HG + gg * HG, HG)], HD), ALU.mult)
                st = state[:, ds(j * 2 * GW + gg * GW, GW)]
                dve.wait_ge(y_ready, n + 1)
                dve.tensor_tensor(y3, ybank[:, GW:2 * GW].rearrange("p (h d) -> p h d", h=HG),
                                  spread(heads(eacum, t, j, gg), HD), ALU.mult)
                dve.tensor_tensor(st.rearrange("p (h d) -> p h d", h=HG), st.rearrange("p (h d) -> p h d", h=HG),
                                  spread(heads(cdec, t, j, gg), HD), ALU.mult)
                dve.drain()
                dve.tensor_tensor(yt1[:, :], yt1[:, :], ybank[:, 0:GW], ALU.add).then_inc(y_free, 1)
                dve.wait_ge(st_ready, n + 1)
                dve.tensor_tensor(st, st, stbank[:, 0:GW], ALU.add).then_inc(st_used, 1)
                yield
                dve.drain()
                dve.tensor_tensor(yt1[:, :], yt1[:, :], yt2[:, :], ALU.add)
                dve.drain()
                y = yg[:, t, gg * GW:(gg + 1) * GW]
                dve.tensor_tensor(y, yt1[:, :], zs[:, t, gg * GW:(gg + 1) * GW], ALU.mult)
                dve.drain()
                dve.tensor_tensor_reduce(yt2[:, :], y, y, 1.0, 0.0, ALU.mult, ALU.add, rms[:, s:s + 1])
                yield

            def rms_scale(c, j):
                dve.drain()
                dve.tensor_scalar(rms[:, :], rms[:, :], 1.0 / GW, EPS, ALU.mult, ALU.add).then_inc(rms_in, 1)
                yield
                dve.wait_ge(rms_sqrt, c * AJ + j + 1)
                dve.reciprocal(rmsr[:, :], rms[:, :]).then_inc(rms_rstd, 1)
                yield

            def scan(c, j):
                unturned(dve, c, j * TA + 8)
                yield from scan_pre(c, j, 0)
                for s in range(4):
                    if s < 3:
                        yield from scan_pre(c, j, s + 1)
                    yield from scan_post(c, j, s)
                yield from rms_scale(c, j)

            def front_pair(c, q):
                g = lexp[:, q % 2, :, :].rearrange("p a b -> p (a b)")
                m = mm[:, q % 2, :, :].rearrange("p a b -> p (a b)")
                dst_ = mflat[:, q * 512:(q + 1) * 512]
                emptied(dve, c, AJ * MA + 2 * q + 2)
                dve.tensor_tensor(m, m, g, ALU.mult)
                dve.drain()
                dve.tensor_tensor(dst_, dst_, m, ALU.add).then_inc(pair_merged, 1)
                yield

            def front_w(c):
                emptied(dve, c, AJ * MA + MC + MW)
                dve.wait_ge(xres_ready, (c + 1) * 48)
                for t in range(NT):
                    h = hf[:, t, :]
                    dve.scalar_tensor_tensor(out=h, in0=xres[:, t, :], scalar=ALPHA, in1=h, op0=ALU.mult, op1=ALU.add)
                    dve.drain()
                    yield
                    for a in range(2):
                        dve.bn_stats(stats[:, t, a, :], hf[:, t, a * 512:(a + 1) * 512])
                    dve.drain()
                    dve.bn_aggr(mv[:, t, :], stats[:, t, :, :])
                    yield
                dve.drain()
                dve.tensor_scalar(lstd[:, :], mv[:, :, 1], EPS, None, ALU.add).then_inc(ln1_var, 1)
                dve.wait_ge(ln1_std, c + 1)
                dve.reciprocal(lrst[:, :], lstd[:, :])
                for t in range(NT):
                    h = hf[:, t, :]
                    dve.drain()
                    dve.tensor_scalar(h, h, mv[:, t, 0:1], lrst[:, t:t + 1], ALU.subtract, ALU.mult)
                    dve.drain()
                    yield
                    dve.tensor_tensor(h, h, lng1, ALU.mult)
                    dve.drain()
                    yield
                    last = dve.tensor_tensor(h, h, lnb1, ALU.add)
                    yield
                last.then_inc(h_ready, 1)
                dve.drain()

            def side_topk(c, i, hh):
                unturned(dve, c, AJ * TA + TW + i * 4 + hh + 1)
                dve.memset(bsum, 0.0)
                for t in range(NT):
                    for side in range(2):
                        u = hh * 2 + t
                        s = ssb[:, hh % 2, t * 2 + side, :]
                        dve.max(tm[:, u, side, 0:8], s)
                        dve.drain()
                        dve.max_index(tmi[:, u, side, 0:8], tm[:, u, side, 0:8], s)
                        dve.match_replace(snext, tm[:, u, side, 0:8], s, LOWEST)
                        dve.drain()
                        dve.max(tm[:, u, side, 8:16], snext)
                        dve.drain()
                        last = dve.max_index(tmi[:, u, side, 8:16], tm[:, u, side, 8:16], snext)
                        yield
                last.then_inc(topk_done, 1)

            def candidates():
                dve.drain()
                dve.tensor_copy(tf, tmi[:, :, :, :])
                dve.drain()
                dve.tensor_scalar(tf[:, :, 0, :], tf[:, :, 0, :], float(KEYS), None, ALU.mult)
                dve.drain()
                for src, dst_ in ((tm, cand), (tf, candi)):
                    at = 0
                    for a in range(5):
                        n = TOPK // (a + 1)
                        dve.tensor_tensor(dst_[:, :, at:at + n], src[:, :, 1, 0:n],
                                          src[:, :, 0, a:a + 1].to_broadcast([P, 8, n]), ALU.add)
                        at += n
                    for a in range(5, 8):
                        dve.tensor_tensor(dst_[:, :, at:at + 2], src[:, :, 1, 0:2],
                                          src[:, :, 0, a:a + 1].to_broadcast([P, 8, 2]), ALU.add)
                        at += 2
                    dve.tensor_tensor(dst_[:, :, at:at + 8], src[:, :, 0, 8:16],
                                      src[:, :, 1, 0:1].to_broadcast([P, 8, 8]), ALU.add)
                    yield
                dve.drain()
                for u in range(8):
                    s = cand[:, u, :]
                    dve.max(bm[:, u, 0:8], s)
                    dve.drain()
                    dve.max_index(pos[:, u, 0:8], bm[:, u, 0:8], s)
                    dve.match_replace(cnext, bm[:, u, 0:8], s, LOWEST)
                    dve.drain()
                    dve.max(bm[:, u, 8:16], cnext)
                    dve.drain()
                    dve.max_index(pos[:, u, 8:16], bm[:, u, 8:16], cnext)
                    if u % 2:
                        yield
                dve.drain()
                dve.tensor_copy(posf, pos[:, :, :])
                dve.tensor_tensor(bex, bm, bm[:, :, 0:1].to_broadcast([P, 8, TOPK]), ALU.subtract).then_inc(sm_in, 1)
                dve.drain()
                yield

            def choose(c, i):
                for u in range(8):
                    for k in range(TOPK):
                        dve.scalar_tensor_tensor(out=sel1[:, k, :], in0=iota[:, :], scalar=posf[:, u, k:k + 1],
                                                 in1=candi[:, u, :], op0=ALU.is_equal, op1=ALU.mult,
                                                 accum_out=self_[:, u, k:k + 1])
                        if k == 7:
                            yield
                    dve.drain()
                    yield
                dve.wait_ge(sm_exp, c * 2 + i + 1)
                dve.tensor_reduce(bsum, bex, AX.X, ALU.add)
                dve.drain()
                dve.reciprocal(bsum, bsum)
                dve.drain()
                for t in range(NT):
                    to = ds(t * PH + i * 4, 4)
                    dve.tensor_copy(idxf[:, to, :], self_[:, t:8:2, :])
                    dve.tensor_tensor(gatef[:, to, :], bex[:, t:8:2, :],
                                      spread(bsum.rearrange("p (h t) -> p h t", t=NT)[:, :, t], TOPK), ALU.mult)
                dve.drain()
                yield

            def front_d(c, i, quarter):
                if quarter < 2:
                    yield from side_topk(c, i, 2 * quarter)
                    yield from side_topk(c, i, 2 * quarter + 1)
                elif quarter == 2:
                    yield from candidates()
                else:
                    yield from choose(c, i)

            def take_over():
                dve.tensor_copy(idxp[:, 0:UNITS, :], idxf[:, :, :])
                dve.tensor_copy(gatep[:, :, :], gatef[:, :, :])
                dve.tensor_copy(hp[:, :, :], hf[:, :, :])
                dve.drain()

            def next_indices(u, b):
                dve.tensor_copy(icur[b][:, :].unsqueeze(1), idxp[:, ds(u, 1), :]).then_inc(idx_ready, 1)

            def dots(c, t, u, b):
                for k in range(TOPK):
                    dve.wait_ge(row_ready[k % ROWS], ((c * UNITS + u) * TURNS_OF_ROWS + k // ROWS + 1) * 16)
                    r = rows[k % ROWS][:, :]
                    last = dve.tensor_tensor_reduce(r, r, hp[:, t, :], 1.0, 0.0, ALU.mult, ALU.add, hdot[:, b, k:k + 1])
                    last.then_inc(row_free, 1)
                    yield

            def sums(c, u, b):
                dve.wait_ge(gelu_ready, c * UNITS + u + 1)
                dve.tensor_tensor(hact[:, b:b + 1, :], hgel[:, b:b + 1, :], gatep[:, ds(u, 1), :], ALU.mult).then_inc(hact_ready, 1)
                for n, k in enumerate(DVE_ROWS, start=TOPK):
                    dve.drain()
                    if k == DVE_ROWS[-1]:
                        for i in range(VPE):
                            dve.wait_ge(row_ready_pe[i], (c * UNITS + u + 1) * 16)
                    dve.wait_ge(row_ready[n % ROWS], ((c * UNITS + u) * TURNS_OF_ROWS + n // ROWS + 1) * 16)
                    dve.scalar_tensor_tensor(out=acc[:, :], in0=rows[n % ROWS][:, :], scalar=hact[:, b, k:k + 1],
                                             in1=acc[:, :], op0=ALU.mult, op1=ALU.add).then_inc(row_free, 1)
                    yield

            def start_tile(c, t):
                dve.wait_ge(out_done, (c * NT + t + 1) * 16)
                dve.tensor_scalar(acc[:, :], hp[:, t, :], ALPHA, None, ALU.mult)

            def finish_tile(c, t):
                dve.drain()
                dve.wait_ge(row_free_pe, (c * UNITS + (t + 1) * PH) * VPE + VPE)
                for half in range(2):
                    o = acc[:, half * 512:(half + 1) * 512]
                    last = dve.tensor_tensor(o, o, vbank[half][:, :], ALU.add)
                last.then_inc(vsum_read, 1)
                dve.drain()
                for a in range(2):
                    dve.bn_stats(pstats[:, a, :], acc[:, a * 512:(a + 1) * 512])
                dve.drain()
                dve.bn_aggr(pmv[:, :], pstats[:, :, :])
                dve.drain()
                dve.tensor_scalar(pstd[:, :], pmv[:, 1:2], EPS, None, ALU.add).then_inc(ln2_var, 1)
                dve.wait_ge(ln2_std, c * NT + t + 1)
                dve.reciprocal(prst[:, :], pstd[:, :])
                dve.drain()
                dve.tensor_scalar(acc[:, :], acc[:, :], pmv[:, 0:1], prst[:, :], ALU.subtract, ALU.mult)
                dve.drain()
                dve.tensor_tensor(acc[:, :], acc[:, :], lng2[:, :], ALU.mult)
                dve.drain()
                dve.tensor_tensor(acc[:, :], acc[:, :], lnb2[:, :], ALU.add).then_inc(out_ready, 1)

            def none():
                return iter(())

            def superchunk(cf, cp, first=False):
                f, e = cf is not None, cp is not None
                if e:
                    take_over()
                if e:
                    start_tile(cp, 0)
                with dve.Fori(0, AJ) as j:
                    for b in range(2):
                        if e:
                            next_indices(j * 2 + b + 1, 1 - b)
                        weave(dots(cp, 0, j * 2 + b, b) if e else none(), pooling(cf, j, first) if f and b == 0 else none(), after=8)
                        weave(sums(cp, j * 2 + b, b) if e else none(),
                              (scan if b else merge_pool)(cf, j) if f else none(), 2 if b else 1, after=0 if b else 2)
                if e:
                    finish_tile(cp, 0)
                for i in range(2):
                    if e:
                        next_indices(9 + i, 1 - i)
                    weave(dots(cp, 1, 8 + i, i) if e else none(), front_pair(cf, 2 * i) if f else none(), after=14)
                    if e and i == 0:
                        start_tile(cp, 1)
                    weave(sums(cp, 8 + i, i) if e else none(), front_pair(cf, 2 * i + 1) if f else none(), after=10)
                if e:
                    next_indices(11, 1)
                w = front_w(cf) if f else none()
                weave(dots(cp, 1, 10, 0) if e else none(), w, after=12, rest=False)
                weave(sums(cp, 10, 0) if e else none(), w, 2)
                if e:
                    next_indices(12, 0)
                weave(dots(cp, 1, 11, 1) if e else none(), front_dt(cf + 1) if f else none(), after=1)
                weave(sums(cp, 11, 1) if e else none(), none())
                with dve.Fori(0, 2) as i:
                    if e:
                        dve.tensor_copy(idxp[:, UNITS, :], idxf[:, 0, :])
                        dve.drain()
                    for b in range(2):
                        if e:
                            next_indices(13 + i * 2 + b, 1 - b)
                        weave(dots(cp, 1, 12 + i * 2 + b, b) if e else none(), front_d(cf, i, 2 * b) if f else none())
                        weave(sums(cp, 12 + i * 2 + b, b) if e else none(), front_d(cf, i, 2 * b + 1) if f else none())
                if e:
                    finish_tile(cp, 1)

            dve.sem_inc(m_done, 2)
            dve.sem_inc(y_free, 1)
            dve.sem_inc(st_used, STATE)
            dve.sem_inc(topk_done, 2)
            dve.sem_inc(row_free, ROWS)
            dve.sem_inc(vsum_read, 1)
            dve.memset(zeros[:, :], 0.0)
            dve.memset(pcoef[:, :, :], 0.0)
            dve.memset(ctail[:, :, :], 0.0)
            dve.memset(ptail[:, :, :], 0.0)
            dve.memset(state[:, :], 0.0)
            dve.drain()
            for w in range(4):
                dve.memset(pcoef[:, w, w:w + 1], 1.0 / WINDOWS[w])
            dve.wait_ge(const_made, 11)
            for w in range(4):
                dve.tensor_scalar(pfix[:, w, :], pfix[:, w, :], float(WINDOWS[w]), None, ALU.min)
            dve.drain()
            dve.reciprocal(pfix[:, :, :], pfix[:, :, :])
            dve.drain()
            for w in range(4):
                dve.tensor_scalar(pfix[:, w, :], pfix[:, w, :], float(WINDOWS[w]), None, ALU.mult)
            dve.wait_ge(const_dma, 16 * NCONST)
            dve.wait_ge(a_made, 1)
            dve.tensor_scalar(a_s[:, :], a_s[:, :], -1.0, None, ALU.mult).then_inc(dve_ready, 1)
            dve.drain()
            for _ in front_dt(0):
                pass
            superchunk(0, None, first=True)
            dve.tensor_copy(icur[0][:, :], idxf[:, 0, :]).then_inc(idx_ready, 1)
            with dve.Fori(0, NC - 1) as c:
                superchunk(c + 1, c)
            superchunk(None, NC - 1)


_OUT = (1, SEQ, D)


def kernel(**inputs):
    import numpy as np
    import concourse.bacc as bacc
    from concourse.bass_utils import run_bass_kernel_spmd

    a = {k: np.asarray(v) for k, v in inputs.items()}
    w_in = a["w_in"][0]
    at = {"pool": 0, "z": D, "x": D + INNER, "B": D + 2 * INNER, "C": D + 2 * INNER + D,
          "dt": 2 * D + INNER * 2 + D, "gp": 2 * D + INNER * 2 + D + HEADS, "gs": 3 * D + INNER * 2 + D + HEADS}

    def blk(w, col):
        return w[:, col:col + 256].reshape(KD, P, 256).transpose(1, 0, 2).reshape(P, KD * 256)

    blocks = []
    for j in range(AJ):
        blocks += [blk(w_in, at["pool"] + 256 * j), blk(w_in, at["gp"] + 256 * j), blk(w_in, at["x"] + 512 * j),
                   blk(w_in, at["x"] + 512 * j + 256), blk(w_in, at["B"] + 256 * j), blk(w_in, at["C"] + 256 * j),
                   blk(w_in, at["z"] + 512 * j), blk(w_in, at["z"] + 512 * j + 256)]
    so = a["ssm_out"][0]
    for q in range(4):
        blocks += [blk(w_in, at["gs"] + 256 * q), blk(so[0:D], 256 * q), blk(so[D:], 256 * q)]
    blocks += [blk(a["w_out"][0], 256 * n) for n in range(4)]
    blocks += [blk(a["w_q"][0], 256 * n) for n in range(PH)]

    def by_block(v):
        v = v.reshape(-1, 4096)
        cols = []
        for j in range(AJ):
            for c0 in (512 * j, 512 * j + 256, INNER + 256 * j, INNER + D + 256 * j):
                cols += [v[:, c0:c0 + P], v[:, c0 + P:c0 + 2 * P]]
        return np.stack(cols, 0).transpose(2, 0, 1)

    x = a["x"][0]
    arrays = {
        "x": x,
        "xt": x.T.reshape(KD, P, SEQ).transpose(1, 0, 2),
        "wblocks": np.stack(blocks),
        "wdt": w_in[:, at["dt"]:at["dt"] + HEADS].reshape(KD, P, HEADS).transpose(1, 0, 2),
        "poolw": a["pool_w"][0].reshape(4, 2, P, 256).transpose(0, 2, 1, 3),
        "pscale": a["pool_scale"][0].reshape(KD, P).T,
        "convw": by_block(a["conv_w"][0]),
        "convb": by_block(a["conv_b"][0])[:, :, 0],
        "dtb": a["dt_bias"], "alog": a["a_log"], "dskip": a["d_skip"],
        "normw": a["ssm_norm_w"][0].reshape(INNER // P, P).T,
        "ln1g": a["ln1_g"], "ln1b": a["ln1_b"], "ln2g": a["ln2_g"], "ln2b": a["ln2_b"],
        "subkt": a["sub_keys"][0].transpose(2, 0, 1),
        "eu": a["expert_u"][0], "ev": a["expert_v"][0],
    }
    arrays = {k: np.ascontiguousarray(v) for k, v in arrays.items()}
    nc = bacc.Bacc("TRN2", target_bir_lowering=False, num_devices=1)
    args = [nc.dram_tensor(k, v.shape, mybir.dt.from_np(v.dtype), kind="ExternalInput").ap() for k, v in arrays.items()]
    args.append(nc.dram_tensor("h_out", (SEQ, D), F32, kind="ExternalOutput").ap())
    build(nc, *args)
    r = run_bass_kernel_spmd(nc, [arrays], core_ids=[0])
    return np.asarray(r.results[0]["h_out"]).reshape(_OUT)
```
